# Optimizing a Trainium2 kernel written in Bass

```python
import jax, jax.numpy as jnp
from jax import lax
import numpy as np

D_MODEL = 1024
BATCH = 1
SEQ = 1024
DEPTH = 1
DEC_BATCH = 8
DEC_SEQ = 1
PAST_LEN = 8192
PAGE_SIZE = 128

MIX_WIDTH = D_MODEL
HGRN_WIDTH = MIX_WIDTH // 2
HGRN_HEADS = 4
HGRN_DK = HGRN_WIDTH // HGRN_HEADS
HGRN_DV = HGRN_WIDTH // HGRN_HEADS
HGRN_CHUNK = 64
POOL_WIDTH = MIX_WIDTH - HGRN_WIDTH
POOL_WINDOWS = (2, 4, 8, 16)
POOL_GROUPS = len(POOL_WINDOWS)
POOL_GROUP_DIM = POOL_WIDTH // POOL_GROUPS
POOL_STATE = max(POOL_WINDOWS) - 1
IN_PROJ = 4 * HGRN_WIDTH + POOL_WIDTH
MEM_LEN = 256
X_HEADS = 4
X_HEAD_DIM = D_MODEL // X_HEADS
D_FF = -(-8 * D_MODEL // (3 * 256)) * 256
EPS = 1e-6

kernel_name = "hgrn2_pool_hybrid_decode_step"

def rmsnorm(x, g):
    xf = x.astype(jnp.float32)
    y = xf * lax.rsqrt(jnp.mean(xf * xf, axis=-1, keepdims=True) + EPS)
    return (y * g.astype(jnp.float32)).astype(x.dtype)

def hgrn2_chunked(q, k, v, logf, s0):
    B, L, H, DK = q.shape
    DV = v.shape[-1]
    C = HGRN_CHUNK if L % HGRN_CHUNK == 0 else L
    n = L // C

    def chunks(a):
        return a.reshape(B, n, C, H, a.shape[-1]).transpose(1, 0, 3, 2, 4)

    causal = jnp.tril(jnp.ones((C, C), dtype=bool))
    mid = (C - 1) // 2

    def step(S, inp):
        qc, kc, vc, lc = inp
        b = jnp.cumsum(lc, axis=2)
        m = b[:, :, mid:mid + 1, :]
        inter = jnp.einsum('bhck,bhkv->bhcv', qc * jnp.exp(b), S)
        a = jnp.einsum('bhck,bhsk->bhcs', qc * jnp.exp(b - m), kc * jnp.exp(m - b))
        intra = jnp.einsum('bhcs,bhsv->bhcv', jnp.where(causal, a, 0.0), vc)
        b_end = b[:, :, -1:, :]
        S = jnp.exp(b_end[:, :, 0, :])[..., None] * S + jnp.einsum(
            'bhck,bhcv->bhkv', kc * jnp.exp(b_end - b), vc)
        return S, inter + intra

    S, o = lax.scan(step, s0, (chunks(q), chunks(k), chunks(v), chunks(logf)))
    return o.transpose(1, 0, 3, 2, 4).reshape(B, L, H, DV), S

def multiscale_pool(u, past, start_pos):
    B, L, _ = u.shape
    P = POOL_STATE
    ext = jnp.concatenate([past.astype(jnp.float32), u.astype(jnp.float32)], axis=1)
    cs = jnp.concatenate([jnp.zeros((B, 1, POOL_WIDTH), jnp.float32),
                          jnp.cumsum(ext, axis=1)], axis=1)
    pos = start_pos + jnp.arange(L)
    outs = []
    for g, w in enumerate(POOL_WINDOWS):
        sl = slice(g * POOL_GROUP_DIM, (g + 1) * POOL_GROUP_DIM)
        hi = cs[:, P + 1:P + 1 + L, sl]
        lo = cs[:, P + 1 - w:P + 1 - w + L, sl]
        cnt = jnp.minimum(pos + 1, w).astype(jnp.float32)[None, :, None]
        outs.append((hi - lo) / cnt)
    return jnp.concatenate(outs, axis=-1) - u.astype(jnp.float32)

def mem_kv(mem, g, w_kv):
    B, M, _ = mem.shape
    kv = rmsnorm(mem, g) @ w_kv
    k, v = jnp.split(kv, 2, axis=-1)
    return (k.reshape(B, M, X_HEADS, X_HEAD_DIM), v.reshape(B, M, X_HEADS, X_HEAD_DIM))

def cross_attend(h, mk, mv, w_q, w_o):
    B, L, _ = h.shape
    q = (h @ w_q).reshape(B, L, X_HEADS, X_HEAD_DIM)
    s = jnp.einsum('blhd,bmhd->bhlm', q.astype(jnp.float32), mk.astype(jnp.float32)) * (X_HEAD_DIM ** -0.5)
    p = jax.nn.softmax(s, axis=-1)
    o = jnp.einsum('bhlm,bmhd->blhd', p, mv.astype(jnp.float32))
    return o.reshape(B, L, D_MODEL).astype(h.dtype) @ w_o

def run_trunk(x, s_hgrn, s_pool, mem_k, mem_v, start_pos, lb_all, g_mix, w_in, hgrn_norm,
              pool_mix, pool_scale, w_out, g_cross, w_cq, w_co, g_ffn, w_ffn_in, w_ffn_out, g_final):
    B, L, _ = x.shape
    new_h, new_p = [], []
    for l in range(DEPTH):
        h = rmsnorm(x, g_mix[l])
        proj = h @ w_in[l]
        qr, fr, ir, gr, u = jnp.split(
            proj, [HGRN_WIDTH, 2 * HGRN_WIDTH, 3 * HGRN_WIDTH, 4 * HGRN_WIDTH], axis=-1)
        lb = lb_all[l]
        zf = fr.astype(jnp.float32)
        logf = jnp.log(lb + (1.0 - lb) * jax.nn.sigmoid(zf))
        kk = (1.0 - lb) * jax.nn.sigmoid(-zf)
        qq = jax.nn.silu(qr.astype(jnp.float32))
        shp = (B, L, HGRN_HEADS, HGRN_DK)
        o, S = hgrn2_chunked(qq.reshape(shp), kk.reshape(shp),
                             ir.astype(jnp.float32).reshape(B, L, HGRN_HEADS, HGRN_DV),
                             logf.reshape(shp), s_hgrn[l].astype(jnp.float32))
        o = o * lax.rsqrt(jnp.mean(o * o, axis=-1, keepdims=True) + EPS)
        o = o * hgrn_norm[l].astype(jnp.float32).reshape(HGRN_HEADS, HGRN_DV)
        y_a = o.reshape(B, L, HGRN_WIDTH) * jax.nn.sigmoid(gr.astype(jnp.float32))
        new_h.append(S.astype(x.dtype))
        past = s_pool[l].astype(u.dtype)
        pooled = multiscale_pool(u, past, start_pos)
        y_b = jnp.einsum('blgc,gcd->blgd',
                         pooled.reshape(B, L, POOL_GROUPS, POOL_GROUP_DIM),
                         pool_mix[l].astype(jnp.float32)).reshape(B, L, POOL_WIDTH)
        y_b = y_b * pool_scale[l].astype(jnp.float32)
        new_p.append(jnp.concatenate([past, u], axis=1)[:, -POOL_STATE:].astype(x.dtype))
        x = x + jnp.concatenate([y_a, y_b], axis=-1).astype(x.dtype) @ w_out[l]
        x = x + cross_attend(rmsnorm(x, g_cross[l]), mem_k[l], mem_v[l], w_cq[l], w_co[l])
        a, bgate = jnp.split(rmsnorm(x, g_ffn[l]) @ w_ffn_in[l], 2, axis=-1)
        x = x + (jax.nn.silu(a) * bgate) @ w_ffn_out[l]
    return rmsnorm(x, g_final), jnp.stack(new_h), jnp.stack(new_p)

def setup_inputs(seed: int = 0) -> dict:
    key = jax.random.key(seed)
    ks = jax.random.split(key, 24)
    f32 = jnp.float32
    nrm = lambda k, s, sc: jax.random.normal(k, s, f32) * sc
    gain = lambda k, s: 1.0 + 0.02 * jax.random.normal(k, s, f32)
    return {
        "x_prompt": nrm(ks[0], (BATCH, SEQ, D_MODEL), 1.0),
        "x_sample": nrm(ks[1], (DEC_BATCH, DEC_SEQ, D_MODEL), 1.0),
        "mem_prompt": nrm(ks[2], (BATCH, MEM_LEN, D_MODEL), 1.0),
        "state_hgrn": nrm(ks[3], (DEPTH, DEC_BATCH, HGRN_HEADS, HGRN_DK, HGRN_DV), 0.3),
        "state_pool": nrm(ks[4], (DEPTH, DEC_BATCH, POOL_STATE, POOL_WIDTH), 1.0),
        "cache_mem_k": nrm(ks[5], (DEPTH, DEC_BATCH, MEM_LEN, X_HEADS, X_HEAD_DIM), 1.0),
        "cache_mem_v": nrm(ks[6], (DEPTH, DEC_BATCH, MEM_LEN, X_HEADS, X_HEAD_DIM), 1.0),
        "g_mix": gain(ks[7], (DEPTH, D_MODEL)),
        "w_in": nrm(ks[8], (DEPTH, D_MODEL, IN_PROJ), D_MODEL ** -0.5),
        "hgrn_lb": nrm(ks[9], (DEPTH + 1, HGRN_WIDTH), 0.1),
        "hgrn_norm": gain(ks[10], (DEPTH, HGRN_WIDTH)),
        "pool_mix": nrm(ks[11], (DEPTH, POOL_GROUPS, POOL_GROUP_DIM, POOL_GROUP_DIM), POOL_GROUP_DIM ** -0.5),
        "pool_scale": gain(ks[12], (DEPTH, POOL_WIDTH)),
        "w_out": nrm(ks[13], (DEPTH, MIX_WIDTH, D_MODEL), MIX_WIDTH ** -0.5),
        "g_mem": gain(ks[14], (DEPTH, D_MODEL)),
        "w_mem_kv": nrm(ks[15], (DEPTH, D_MODEL, 2 * D_MODEL), D_MODEL ** -0.5),
        "g_cross": gain(ks[16], (DEPTH, D_MODEL)),
        "w_cq": nrm(ks[17], (DEPTH, D_MODEL, D_MODEL), D_MODEL ** -0.5),
        "w_co": nrm(ks[18], (DEPTH, D_MODEL, D_MODEL), D_MODEL ** -0.5),
        "g_ffn": gain(ks[19], (DEPTH, D_MODEL)),
        "w_ffn_in": nrm(ks[20], (DEPTH, D_MODEL, 2 * D_FF), D_MODEL ** -0.5),
        "w_ffn_out": nrm(ks[21], (DEPTH, D_FF, D_MODEL), D_FF ** -0.5),
        "g_final": gain(ks[22], (D_MODEL,)),
    }

def reference(x_prompt, x_sample, mem_prompt, state_hgrn, state_pool, cache_mem_k, cache_mem_v,
              g_mix, w_in, hgrn_lb, hgrn_norm, pool_mix, pool_scale, w_out, g_mem, w_mem_kv,
              g_cross, w_cq, w_co, g_ffn, w_ffn_in, w_ffn_out, g_final):
    lb_all = jnp.cumsum(jax.nn.softmax(hgrn_lb.astype(jnp.float32), axis=0), axis=0)
    kv = [mem_kv(mem_prompt, g_mem[l], w_mem_kv[l]) for l in range(DEPTH)]
    new_mem_k = jnp.stack([p[0] for p in kv])
    new_mem_v = jnp.stack([p[1] for p in kv])
    s0_hgrn = jnp.zeros((DEPTH, BATCH, HGRN_HEADS, HGRN_DK, HGRN_DV), x_prompt.dtype)
    s0_pool = jnp.zeros((DEPTH, BATCH, POOL_STATE, POOL_WIDTH), x_prompt.dtype)
    y_prompt, hgrn_p, pool_p = run_trunk(
        x_prompt, s0_hgrn, s0_pool, new_mem_k, new_mem_v, 0, lb_all, g_mix, w_in, hgrn_norm,
        pool_mix, pool_scale, w_out, g_cross, w_cq, w_co, g_ffn, w_ffn_in, w_ffn_out, g_final)
    y_sample, hgrn_s, pool_s = run_trunk(
        x_sample, state_hgrn, state_pool, cache_mem_k, cache_mem_v, PAST_LEN, lb_all, g_mix, w_in,
        hgrn_norm, pool_mix, pool_scale, w_out, g_cross, w_cq, w_co, g_ffn, w_ffn_in, w_ffn_out, g_final)
    return (y_prompt, y_sample, hgrn_p, pool_p, new_mem_k, new_mem_v, hgrn_s, pool_s)


_drawn_inputs = setup_inputs


def setup_inputs(seed=0):
    import zlib

    import numpy as np

    out = dict(_drawn_inputs(seed))
    spreads = {}
    factors = {'hgrn_norm': 8.0,
     'pool_scale': 5.286,
     'g_mem': 2.876,
     'g_cross': 8.0,
     'g_ffn': 4.561,
     'g_final': 2.816}
    for name, (base, spread) in spreads.items():
        noise = np.random.default_rng([zlib.crc32(name.encode()), seed]).standard_normal(out[name].shape)
        drawn = base * np.exp(spread * noise) if base else spread * noise
        out[name] = __import__('jax').numpy.asarray(drawn.astype(out[name].dtype))
    for name, factor in factors.items():
        out[name] = (out[name] * factor).astype(out[name].dtype)
    return out
```

```python
from contextlib import ExitStack

import numpy as np

import concourse.bass as bass
from concourse import mybir
from concourse.alu_op_type import AluOpType as ALU

ACT = mybir.ActivationFunctionType
F32 = mybir.dt.float32
F32R = mybir.dt.float32r
I32 = mybir.dt.int32
AX_X = mybir.AxisListType.X

P = 128
D = 1024
KB = D // P
TP = 1024
NS = 8
T = TP + NS
CH = 344
NC = T // CH
H = 4
W = 512
C = 64
MID = (C - 1) // 2
PAIRS = TP // (2 * C)
POOLW = (2, 4, 8, 16)
PAST = 15
M = 256
XD = 256
FF = 2816
FB = FF // P
GROUPS = ((0, 8), (8, 8), (16, 6))
EPS = 1e-6
SCALE = XD ** -0.5


class Phase:

    def __init__(self, name, stripes, chunks, gain):
        self.name, self.stripes, self.chunks, self.gain = name, stripes, chunks, gain
        self.first = self.done = self.scaled = None


def make_phases():
    ph = [Phase("qfi", 12, NC, 0), Phase("gu", 8, NC, 0), Phase("out", 8, NC, None), Phase("cq", 8, NC, 1),
          Phase("kv", 16, 1, None), Phase("co", 8, NC, None)]
    for f0, fb in GROUPS:
        ph += [Phase(f"in{f0}", 2 * fb, NC, 2), Phase(f"down{f0}", 8, NC, None)]
    n, done, scaled = 0, 4, 0
    for p in ph:
        p.first, p.done, p.scaled = n, done, scaled
        n += p.stripes
        done += p.stripes * p.chunks
        scaled += p.stripes if p.gain is not None else 0
    return ph


def hybrid_layer(nc, t, stop=None):
    t = {name: ap[0] if name in PER_LAYER else ap for name, ap in t.items()}
    phases = make_phases()
    ph = {p.name: p for p in phases}
    after = {a.name: b for a, b in zip(phases, phases[1:])}

    with ExitStack() as ctx:
        def sem(name):
            return ctx.enter_context(nc.semaphore(name))

        base = 16512
        spot = [base]

        def put(name, shape, dt=F32, at=None):
            free = int(np.prod(shape[1:])) * 4
            off = spot[0] if at is None else at
            if at is None:
                spot[0] += (free + 31) // 32 * 32
            assert off + free <= 229344, (name, off + free)
            return nc.alloc_sbuf_tensor_at(name, list(shape), dt, offset=off)

        x_hi = put("x_hi", [P, KB, T], F32R)
        x_lo = put("x_lo", [P, KB, T], F32R)
        raw = put("raw", [P, 2, KB, P])
        w_hi = [put(f"w_hi{s}", [P, KB, P], F32R) for s in range(2)]
        w_lo = [put(f"w_lo{s}", [P, KB, P], F32R) for s in range(2)]
        ident = put("ident", [P, P])
        ones = put("ones", [P, P])
        cmask = put("cmask", [P, P], I32)
        cmaskf = put("cmaskf", [P, P])
        keep = put("keep", [P, W])
        rb = put("rb", [P, T])
        gains = put("gains", [P, 3, KB])
        gmem = put("gmem", [P, KB])
        lbt = put("lbt", [P, 2, H])
        lbw = put("lbw", [P, 4, H])
        omlb = put("omlb", [P, H])
        hnorm = put("hnorm", [P, H])
        pscale = put("pscale", [P, H])
        ss = put("ss", [P, 16])
        eps = put("eps", [P, 1])
        pad = put("pad", [P, 4])
        rtok = put("rtok", [P, 16])
        fac = put("fac", [P, 16])
        r0 = spot[0]
        Z = T * 4

        proj = put("proj", [P, 20, T], at=r0)
        q_, f_, i_, g_, u_ = (proj[:, 4 * n:4 * n + 4, :] for n in range(5))
        y_lo = put("y_lo", [P, KB, T], F32R, at=r0)
        y_hi = put("y_hi", [P, KB, T], F32R, at=r0 + 8 * Z)
        r1 = r0 + 20 * Z
        o0 = r1
        names = ["lf", "b", "d", "e1", "e2", "e3a", "e3b", "e4", "iv", "kt", "vt", "am", "S0", "S1"]
        hg = {}
        for n in names:
            hg[n] = put(n, [P, H, P], at=o0)
            o0 += 2048
        ebs = put("ebs", [P, 2, H, 2], at=o0)
        assert o0 + 64 <= 229344
        s_old = [put(f"s_old{n}", [P, H, P], at=r1 + n * 2048) for n in range(2)]
        s_new = [put(f"s_new{n}", [P, H, P], at=r1 + 4096 + n * 2048) for n in range(2)]
        osq = put("osq", [P, T], at=r1)
        orr = put("orr", [P, T], at=r1 + Z)
        o1 = r1 + 2 * Z
        pa = put("pa", [P, TP], at=o1)
        pb = put("pb", [P, TP], at=o1 + 4096)
        pastT = put("pastT", [P, H, NS * PAST], at=o1 + 8192)
        psums = put("psums", [P, H, NS], at=o1 + 8192 + 1920)
        fs = put("fs", [P, H, NS], at=o1 + 8192 + 2048)
        past = put("past", [P, W], at=o1 + 8192 + 2176)
        utok = put("utok", [32, W], at=o1 + 8192 + 2176 + 2048)
        assert o1 + 8192 + 2176 + 4096 <= r1 + 12 * 2048
        pmix = put("pmix", [P, H, P], at=r1 + 13 * 2048)

        r2 = r0 + 16 * Z
        sqacc = put("sqacc", [P, T], at=r2)
        xnew = put("xnew", [P, 2, CH], at=r2 + Z)
        xsq = put("xsq", [P, 2, CH], at=r2 + Z + 2 * CH * 4)

        qT = put("qT", [P, KB, T], at=r0)
        o_lo = put("o_lo", [P, KB, T], F32R, at=r0)
        o_hi = put("o_hi", [P, KB, T], F32R, at=r0 + 8 * Z)
        g2 = r0 + 8 * Z
        m_hi = put("m_hi", [P, KB, M], F32R, at=g2)
        m_lo = put("m_lo", [P, KB, M], F32R, at=g2 + 8192)
        mtok = put("mtok", [P, 2, D], at=g2 + 16384)
        mf = put("mf", [P, KB, P], at=g2 + 24576)
        mjunk = put("mjunk", [P, D], at=g2 + 28672)
        knat = put("knat", [P, 2, D], at=g2 + 16384)
        kvT = put("kvT", [P, 16, M], at=r2)
        vnat = put("vnat", [P, 2, D], at=r2 + 16384)
        rbm = put("rbm", [P, M], at=r2 + 24576 + 12288)
        qs = put("qs", [P, KB, P], at=r2 + 24576)
        pr = put("pr", [P, H, XD], at=r2 + 24576 + 4096)
        prT = put("prT", [P, KB, P], at=r2 + 24576 + 8192)
        smax = put("smax", [P, H], at=r2 + 24576 + 13312)
        nmax = put("nmax", [P, H], at=r2 + 24576 + 13312 + 32)
        den = put("den", [P, H], at=r2 + 24576 + 13312 + 64)
        rden = put("rden", [P, H], at=r2 + 24576 + 13312 + 96)
        kc = [put(f"kc{n}", [P, 2, D], at=r2 + n * 8192) for n in range(2)]
        vc = [put(f"vc{n}", [P, 2, D], at=r2 + 16384 + n * 8192) for n in range(2)]
        ssc = put("ssc", [P, 2, NS * H], at=r2 + 32768)
        sp_ = put("sp_", [32, 2, P], at=r2 + 33024)
        spT = put("spT", [P, 2, NS * H], at=r2 + 34048)
        sst = put("sst", [32, 8], at=r2 + 34304)

        s_lo = put("s_lo", [P, KB, T], F32R, at=r0)
        s_hi = put("s_hi", [P, KB, T], F32R, at=r0 + 8 * Z)
        acc = put("acc", [P, KB, T], at=r2)
        r3 = r0 + 24 * Z
        fa = put("fa", [P, T], at=r3)
        fp = put("fp", [P, 2, CH], at=r3 + Z)
        gfin = put("gfin", [P, D], at=r0)
        ytok = [put(f"ytok{n}", [P, D], at=r0 + 4096 * (n + 1)) for n in range(2)]
        yjunk = put("yjunk", [P, D], at=r0 + 4096 * 3)

        xt = [put(f"xt{n}", [P, D], at=r0 + n * 4096) for n in range(9)]
        junk = put("junk", [P, D], at=r0 + 9 * 4096)

        pm = ctx.enter_context(nc.psum_tensor("pm", [P, 8, 512], F32))
        bank = [pm[:, b, :] for b in range(8)]

        def wide(b0, n=2):
            return pm[:, b0:b0 + n, :].rearrange("p b c -> p (b c)")

        raw_in = [sem(f"raw_in{s}") for s in range(2)]
        gain_on = sem("gain_on")
        hi_made = sem("hi_made")
        lo_made = sem("lo_made")
        mm_done = sem("mm_done")
        evac = sem("evac")
        const_in = sem("const_in")
        gmix_in = sem("gmix_in")
        setup = sem("setup")
        chain = sem("chain")
        x_in = [sem(f"x_in{n}") for n in range(9)]
        x_turned = sem("x_turned")
        x_split = sem("x_split")
        x_sq = sem("x_sq")
        r_made = sem("r_made")
        r_wide = sem("r_wide")
        rb_made = sem("rb_made")
        q_act = sem("q_act")
        k_act = sem("k_act")
        lf_made = sem("lf_made")
        b_made = sem("b_made")
        d_made = sem("d_made")
        e_made = sem("e_made")
        exp_d = sem("exp_d")
        exp_e = sem("exp_e")
        exp_b = sem("exp_b")
        qk_made = sem("qk_made")
        kn_made = sem("kn_made")
        qb_made = sem("qb_made")
        iv_made = sem("iv_made")
        turned = sem("turned")
        kv_out = sem("kv_out")
        ap_done = sem("ap_done")
        masked = sem("masked")
        S1_made = sem("S1_made")
        S0_made = sem("S0_made")
        o_done = sem("o_done")
        o_out = sem("o_out")
        stored = sem("stored")
        g_act = sem("g_act")
        misc_in = sem("misc_in")
        past_in = sem("past_in")
        old_in = [sem(f"old_in{s}") for s in range(2)]
        v_wide = sem("v_wide")
        fs_made = sem("fs_made")
        new_made = sem("new_made")
        new_read = sem("new_read")
        new_out = [sem(f"new_out{s}") for s in range(2)]
        o_all = sem("o_all")
        osq_made = sem("osq_made")
        osum = sem("osum")
        orr_made = sem("orr_made")
        y_step = sem("y_step")
        ya_made = sem("ya_made")
        past_turned = sem("past_turned")
        past_made = sem("past_made")
        u_turned = sem("u_turned")
        utok_made = sem("utok_made")
        pool_step = sem("pool_step")
        pooled = sem("pooled")
        spooled = sem("spooled")
        mixed = sem("mixed")
        yb_hi = sem("yb_hi")
        yb_made = sem("yb_made")
        xsum = sem("xsum")
        xh_made = sem("xh_made")
        xl_made = sem("xl_made")
        sq_made = sem("sq_made")
        sq_added = sem("sq_added")
        sq_wide = sem("sq_wide")
        mem_in = sem("mem_in")
        mem_sq = sem("mem_sq")
        mem_turned = sem("mem_turned")
        mem_step = sem("mem_step")
        rbm_wide = sem("rbm_wide")
        rbm_made = sem("rbm_made")
        kv_turned = sem("kv_turned")
        kv_nat = sem("kv_nat")
        kn_out = sem("kn_out")
        qs_made = sem("qs_made")
        sc_done = sem("sc_done")
        mx_step = sem("mx_step")
        mx_made = sem("mx_made")
        ex_made = sem("ex_made")
        rd_made = sem("rd_made")
        p_made = sem("p_made")
        pt_done = sem("pt_done")
        pt_out = sem("pt_out")
        pv_done = sem("pv_done")
        pv_hi = sem("pv_hi")
        pv_out = sem("pv_out")
        kc_in = [sem(f"kc_in{s}") for s in range(2)]
        vc_in = [sem(f"vc_in{s}") for s in range(2)]
        sq_w = sem("sq_w")
        ssc_made = sem("ssc_made")
        sv_done = sem("sv_done")
        ssc_turned = sem("ssc_turned")
        ssm = sem("ssm")
        sex = sem("sex")
        sp_turned = sem("sp_turned")
        so_made = sem("so_made")
        silu_made = sem("silu_made")
        fprod = sem("fprod")
        s_hi_made = sem("s_hi_made")
        s_made = sem("s_made")
        acc_made = sem("acc_made")
        gfin_in = sem("gfin_in")
        pool_zero = sem("pool_zero")
        y_turned = sem("y_turned")
        yfac = sem("yfac")
        y_made = sem("y_made")
        y_out = [sem(f"y_out{s}") for s in range(2)]
        block = ctx.enter_context(nc.Block())
        stores = [0]

        w_src = {"qfi": ("w_in", 0), "gu": ("w_in", 12 * P)}

        def stripe_src(p, j, s):
            name = p.name
            if name in ("qfi", "gu"):
                w, off = t["w_in"], (0 if name == "qfi" else 12 * P)
            elif name == "out":
                w, off = t["w_out"], 0
            elif name == "cq":
                w, off = t["w_cq"], 0
            elif name == "kv":
                w, off = t["w_mem_kv"], 0
            elif name == "co":
                w, off = t["w_co"], 0
            elif name.startswith("in"):
                v = t["w_ffn_in"].rearrange("(k p) n -> p k n", p=P)
                return v, int(name[2:]) * P, P, s * FF
            else:
                f0 = int(name[4:])
                fb = dict(GROUPS)[f0]
                v = t["w_ffn_out"][f0 * P:(f0 + fb) * P, :].rearrange("(k p) n -> p k n", p=P)
                return v, 0, 2 * P, s * P
            return w.rearrange("(k p) n -> p k n", p=P), off, 2 * P, s * P

        live = [p for p in phases if stop is None or phases.index(p) < stop]

        @block.sync
        def _(sp):
            def load_stripe(p, i, s, wait=True):
                v, off, step, extra = stripe_src(p, i, s)
                if wait:
                    sp.wait_ge(lo_made, p.first + 2 * i + s - 1)
                kb = v.shape[1]
                src = v[:, :, bass.ds(i * step + (off + extra), P)]
                sp.dma_start(raw[:, s, 0:kb, :], src).then_inc(raw_in[s], 16)

            for n in range(9):
                src = t["x_prompt"][0, n * P:(n + 1) * P, :] if n < 8 else t["x_sample"].rearrange("b o d -> (b o) d")
                rows = P if n < 8 else NS
                sp.dma_start(xt[n][0:rows, :], src).then_inc(x_in[n], 16)
                if n == 2:
                    sp.dma_start(gains[:, 0, :], t["g_mix"].rearrange("(k p) -> p k", p=P),
                         allow_slow_non_contiguous=True).then_inc(gmix_in, 16)
                    load_stripe(phases[0], 0, 0, False)
                    load_stripe(phases[0], 0, 1, False)
            sp.dma_start(gains[:, 1, :], t["g_cross"].rearrange("(k p) -> p k", p=P),
                         allow_slow_non_contiguous=True).then_inc(const_in, 16)
            sp.dma_start(gains[:, 2, :], t["g_ffn"].rearrange("(k p) -> p k", p=P),
                         allow_slow_non_contiguous=True).then_inc(const_in, 16)
            sp.dma_start(gmem[:, :], t["g_mem"].rearrange("(k p) -> p k", p=P),
                         allow_slow_non_contiguous=True).then_inc(const_in, 16)
            sp.dma_start(lbt[:, :, :], t["hgrn_lb"].rearrange("l (h p) -> p l h", p=P),
                         allow_slow_non_contiguous=True).then_inc(const_in, 16)
            sp.dma_start(hnorm[:, :], t["hgrn_norm"].rearrange("(h p) -> p h", p=P),
                         allow_slow_non_contiguous=True).then_inc(const_in, 16)
            sp.dma_start(pscale[:, :], t["pool_scale"].rearrange("(h p) -> p h", p=P),
                         allow_slow_non_contiguous=True).then_inc(const_in, 16)
            for p in live:
                at = 1 if p is phases[0] else 0
                if p.name == "co":
                    at = 1
                if p.name in ("out", "cq", "kv"):
                    load_stripe(p, 0, 0)
                    load_stripe(p, 0, 1)
                    at = 1
                if p.name == "out":
                    sp.wait_ge(o_done, PAIRS + 2)
                    sp.wait_ge(S0_made, PAIRS + 1)
                    sp.dma_start(t["hgrn_prompt"][0].rearrange("h k v -> k h v"), hg["S0"][:, :, :]).then_inc(stored, 16)
                    sp.dma_start(past[0:NS * PAST, :],
                                 t["state_pool"].rearrange("b r c -> (b r) c")).then_inc(past_in, 16)
                    sp.dma_start(pmix[:, :, :], t["pool_mix"].rearrange("g c d -> c g d")).then_inc(misc_in, 16)
                    for b in range(NS):
                        if b >= 2:
                            sp.wait_ge(new_made, 2 * b - 2)
                        sp.dma_start(s_old[b % 2][:, :, :],
                                     t["state_hgrn"][b].rearrange("h k v -> k h v")).then_inc(old_in[b % 2], 16)
                if p.name == "cq":
                    sp.wait_ge(mm_done, p.done)
                    for n in range(2):
                        sp.dma_start(mtok[:, n, :], t["mem_prompt"][0, n * P:(n + 1) * P, :]).then_inc(mem_in, 16)
                with sp.Fori(at, p.stripes // 2) as i:
                    for s in range(2):
                        load_stripe(p, i, s)
                if p.name == "kv":
                    load_stripe(ph["co"], 0, 0)
                    load_stripe(ph["co"], 0, 1)
                    sp.wait_ge(kv_nat, 2)
                    sp.dma_start(t["mem_k"][0].rearrange("(a p) h d -> p a (h d)", p=P), knat[:, :, :]).then_inc(kn_out, 16)
                    sp.wait_ge(kv_nat, 4)
                    sp.dma_start(t["mem_v"][0].rearrange("(a p) h d -> p a (h d)", p=P), vnat[:, :, :]).then_inc(stored, 16)
                    def load_cache(n):
                        if n >= 2:
                            sp.wait_ge(ssc_made, n - 1)
                        sp.dma_start(kc[n % 2][:, :, :], t["cache_mem_k"][n].rearrange(
                            "(a p) h d -> p a (h d)", p=P)).then_inc(kc_in[n % 2], 16)

                    def load_values(n):
                        if n >= 2:
                            sp.wait_ge(sv_done, n - 1)
                        sp.dma_start(vc[n % 2][:, :, :], t["cache_mem_v"][n].rearrange(
                            "(a p) h d -> p a (h d)", p=P)).then_inc(vc_in[n % 2], 16)
                    sp.wait_ge(sc_done, PAIRS)
                    sp.wait_ge(stored, 16 * 5)
                    load_cache(0)
                    load_cache(1)
                    sp.wait_ge(pv_done, PAIRS + 1)
                    load_values(0)
                    load_values(1)
                    for n in range(2, NS):
                        load_cache(n)
                    for n in range(2, NS):
                        load_values(n)
            sp.wait_ge(mm_done, phases[-1].done + 8 * NC)
            sp.dma_start(gfin[:, :], t["g_final"].unsqueeze(0).to_broadcast([P, D])).then_inc(gfin_in, 16)
            for n in range(9):
                rows = P if n < 8 else NS
                sp.wait_ge(y_made, n + 1)
                dst = t["y_prompt"][0, n * P:(n + 1) * P, :] if n < 8 else t["y_sample"].rearrange("b o d -> (b o) d")
                sp.dma_start(dst, ytok[n % 2][0:rows, :]).then_inc(y_out[n % 2], 16)
            sp.wait_ge(y_out[0], 16 * 5)
            sp.wait_ge(y_out[1], 16 * 4)
            sp.wait_ge(new_out[0], 16 * 4)
            sp.wait_ge(new_out[1], 16 * 4)
            sp.wait_ge(kn_out, 16)
            sp.wait_ge(stored, 16 * 5)

        def nxt(p, i, s, last):
            if s == 0:
                return p, i, 1
            if not last:
                return p, i + 1, 0
            q = after.get(p.name)
            return (q, 0, 0) if q in live else None

        def pairs(eng, p, body):
            n = p.stripes // 2
            with eng.Fori(0, n - 1) as i:
                body(i, False)
            body(n - 1, True)

        @block.gpsimd
        def _(pool):
            pool.memset(ident[:, :], 0.0).then_inc(setup, 1)
            pool.wait_ge(setup, 1)
            pool.affine_select(out=ident[:, :], in_=ident[:, :], compare_op=ALU.not_equal, fill=1.0, base=0,
                               pattern=[[-1, P]], channel_multiplier=1).then_inc(setup, 1)
            pool.memset(ones[:, :], 1.0).then_inc(setup, 1)
            pool.memset(cmaskf[:, :], 1.0).then_inc(setup, 1)
            pool.wait_ge(setup, 4)
            pool.affine_select(out=cmaskf[:, :], in_=cmaskf[:, :], compare_op=ALU.is_ge, fill=0.0, base=0,
                               pattern=[[1, P]], channel_multiplier=-1).then_inc(setup, 1)
            pool.wait_ge(setup, 5)
            pool.memset(cmaskf[0:C, C:P], 0.0).then_inc(setup, 1)
            pool.wait_ge(setup, 6)
            pool.tensor_copy(cmask[:, :], cmaskf[:, :]).then_inc(setup, 1)
            pool.memset(keep[:, :], 1.0).then_inc(setup, 1)
            pool.wait_ge(setup, 8)
            pool.memset(keep[:, :].rearrange("p (n c) -> p n c", c=C)[:, :, 0:1], 0.0).then_inc(setup, 1)
            pool.memset(eps[:, :], EPS).then_inc(setup, 1)
            pool.memset(pad[:, :], 0.0).then_inc(sq_made, 2)

            def gain_stripe(p, i, s):
                pool.wait_ge(raw_in[s], p.first * 8 + 16 * i + 16)
                g = gains[:, p.gain, :].unsqueeze(2).to_broadcast([P, KB, P])
                pool.tensor_tensor(raw[:, s, :, :], raw[:, s, :, :], g, ALU.mult).then_inc(gain_on, 1)

            def v_copy(i, s):
                p_ = 2 * i + s
                pool.wait_ge(evac, ph["gu"].done)
                pool.wait_ge(turned, p_ + 1)
                pool.tensor_copy(hg["iv"][:, :, :], i_[:, :, bass.ds(p_ * P, P)]).then_inc(iv_made, 1)

            def pooling():
                steps = [0]

                def step(ins):
                    steps[0] += 1
                    ins.then_inc(pool_step, 1)
                    pool.wait_ge(pool_step, steps[0])

                pool.wait_ge(evac, ph["out"].done)
                pool.wait_ge(o_done, PAIRS + 2)
                pool.wait_ge(u_turned, 1)
                for g, w in enumerate(POOLW):
                    cur = u_[:, g, 0:TP]
                    for l in range(g + 1):
                        dst, sh = (pa, pb)[l % 2][:, :], 1 << l
                        step(pool.tensor_tensor(dst[:, sh:TP], cur[:, sh:TP], cur[:, 0:TP - sh], ALU.add))
                        step(pool.tensor_copy(dst[:, 0:sh], cur[:, 0:sh]))
                        cur = dst
                    for c in range(w - 1):
                        step(pool.tensor_scalar(cur[:, c:c + 1], cur[:, c:c + 1], w / (c + 1.0), None, ALU.mult))
                    step(pool.tensor_scalar(cur, cur, 1.0 / w, None, ALU.mult))
                    pool.tensor_tensor(u_[:, g, 0:TP], cur, u_[:, g, 0:TP], ALU.subtract).then_inc(pooled, 1)
                    pool.wait_ge(pooled, g + 1)

            def squares(p, i, s, c):
                e = 6 * i + 3 * s + c
                at = 0 if p.name == "out" else 8 * NC
                slot = (3 * s + c) % 2
                pool.wait_ge(xsum, at + e + 1)
                pool.wait_ge(setup, 10)
                pool.tensor_tensor(xsq[:, slot, :], xnew[:, slot, :], xnew[:, slot, :], ALU.mult).then_inc(sq_made, 1)
                pool.wait_ge(sq_made, at + e + 3)
                cc = sqacc[:, c * CH:(c + 1) * CH]
                pool.tensor_tensor(cc, cc, xsq[:, slot, :], ALU.add).then_inc(sq_added, 1)
                pool.wait_ge(sq_added, at + e + 1)

            for p in live:
                if p.name == "out":
                    pooling()
                if p.name in ("out", "co"):
                    pool.wait_ge(evac, p.done + 1)
                    pool.memset(sqacc[:, :], 0.0).then_inc(pool_zero, 1)
                    pool.wait_ge(pool_zero, 1 if p.name == "out" else 2)
                    def body(i, last):
                        if last:
                            gain_stripe(after[p.name], 0, 0)
                        for s in range(2):
                            for c in range(NC):
                                squares(p, i, s, c)
                    pairs(pool, p, body)
                if p.gain is None:
                    continue
                if p is phases[0]:
                    pool.wait_ge(gmix_in, 16)
                ahead = p.name in ("cq", "in0")
                if ahead:
                    gain_stripe(p, 0, 1)
                with pool.Fori(1 if ahead else 0, p.stripes // 2) as i:
                    for s in range(2):
                        gain_stripe(p, i, s)
                        if p.name == "gu":
                            v_copy(i, s)

        @block.scalar
        def _(act):
            def split_hi(p, i, s, free):
                act.wait_ge(raw_in[s], p.first * 8 + 16 * i + 16)
                if p.gain is not None:
                    act.wait_ge(gain_on, p.scaled + 2 * i + s + 1)
                if free is not None:
                    act.wait_ge(mm_done, free)
                act.activation(w_hi[s][:, :, :], raw[:, s, :, :], ACT.Copy).then_inc(hi_made, 1)

            def split_next(p, i, s, last):
                n = nxt(p, i, s, last)
                if n:
                    split_hi(*n, free=p.done + 2 * p.chunks * i + s * p.chunks)

            split_hi(phases[0], 0, 0, None)
            act.wait_ge(chain, 1)
            act.wait_ge(setup, 10)
            for n in range(9):
                rows = P if n < 8 else NS
                act.wait_ge(x_in[n], 16)
                if n:
                    act.wait_ge(x_sq, n)
                act.activation(junk[0:rows, :], xt[n][0:rows, :], ACT.Square,
                               accum_out=ss[0:rows, n:n + 1]).then_inc(x_sq, 1)
            act.wait_ge(x_sq, 9)
            act.wait_ge(o_out, 1)
            act.activation(rtok[:, 0:9], ss[:, 0:9], ACT.Ln, scale=1.0 / D, bias=eps[:, 0:1]).then_inc(x_sq, 1)
            act.wait_ge(x_sq, 10)
            act.activation(rtok[:, 0:9], rtok[:, 0:9], ACT.Exp, scale=-0.5).then_inc(r_made, 1)
            act.wait_ge(chain, 3)
            act.activation(lbw[:, 0:2, :], lbt[:, :, :], ACT.Exp).then_inc(r_made, 1)

            p = ph["qfi"]
            for i in range(6):
                for s in range(2):
                    split_next(p, i, s, i == 5)
                if i == 2:
                    act.wait_ge(evac, p.done + 12)
                    act.activation(q_, q_, ACT.Silu).then_inc(q_act, 1)
                if i == 4:
                    act.wait_ge(evac, p.done + 24)
                    act.activation(f_, f_, ACT.Sigmoid, scale=-1.0).then_inc(k_act, 1)
                    act.wait_ge(k_act, 1)
                    act.wait_ge(chain, 6)
                    for h in range(H):
                        act.activation(f_[:, h, :], f_[:, h, :], ACT.Copy, scale=omlb[:, h:h + 1]).then_inc(k_act, 1)

            def gates(i, s):
                n = 2 * i + s
                act.activation(hg["lf"][:, :, :], f_[:, :, bass.ds(n * P, P)], ACT.Ln, scale=-1.0,
                               bias=1.0).then_inc(lf_made, 1)
                act.wait_ge(e_made, n + 1)
                act.wait_ge(turned, n + 1)
                act.activation(hg["e4"][:, :, :], hg["lf"][:, :, :], ACT.Exp).then_inc(exp_e, 1)
                act.wait_ge(o_done, n + 1)
                if not isinstance(n, int) or n:
                    act.wait_ge(S0_made, n)
                act.activation(ebs[:, s, :, :], hg["b"][:, :, C - 1::C], ACT.Exp)
                act.activation(hg["e3a" if s == 0 else "e3b"][:, :, :], hg["b"][:, :, :], ACT.Exp).then_inc(exp_b, 1)
                act.wait_ge(d_made, n + 1)
                act.wait_ge(ap_done, n + 1)
                act.activation(hg["e1"][:, :, :], hg["d"][:, :, :], ACT.Exp)
                act.activation(hg["e2"][:, :, :], hg["d"][:, :, :], ACT.Exp, scale=-1.0).then_inc(exp_d, 1)

            def kv_read(i, s):
                n = 2 * i + s
                act.wait_ge(turned, n + 2)
                act.wait_ge(o_done, n + 2)
                act.activation(hg["kt"][:, :, :], bank[3].rearrange("p (h c) -> p h c", h=H), ACT.Copy)
                act.activation(hg["vt"][:, :, :], bank[4].rearrange("p (h c) -> p h c", h=H),
                               ACT.Copy).then_inc(kv_out, 1)

            act.wait_ge(k_act, 1 + H)
            gates(0, 0)
            p = ph["gu"]

            def gu_body(i, last):
                for s in range(2):
                    split_next(p, i, s, last)
                    kv_read(i, s)
                    n = nxt(p, i, s, last)
                    if n and n[0] is p:
                        gates(n[1], n[2])
            if p in live:
                pairs(act, p, gu_body)

            def mixer_end():
                act.wait_ge(evac, ph["gu"].done + 4 * NC)
                act.activation(g_, g_, ACT.Sigmoid).then_inc(g_act, 1)
                act.wait_ge(past_turned, 1)
                act.wait_ge(o_done, PAIRS + 2)
                act.activation(pastT[:, :, :], bank[5][:, 0:480].rearrange("p (g r) -> p g r", g=H),
                               ACT.Copy).then_inc(past_made, 1)
                act.wait_ge(u_turned, 1)
                act.activation(utok[0:23, :], bank[3][0:23, :], ACT.Copy).then_inc(utok_made, 1)
                act.wait_ge(utok_made, 1)
                act.dma_start(t["pool_prompt"][0], utok[0:PAST, :]).then_inc(stored, 16)
                act.dma_start(t["pool_sample"][:, PAST - 1, :], utok[PAST:PAST + NS, :]).then_inc(stored, 16)
                act.dma_start(t["pool_sample"][:, 0:PAST - 1, :], t["state_pool"][:, 1:PAST, :]).then_inc(stored, 16)
                for b in range(NS):
                    act.wait_ge(new_made, 2 * b + 2)
                    act.dma_start(t["hgrn_sample"][b].rearrange("h k v -> k h v"),
                                  s_new[b % 2][:, :, :]).then_inc(new_out[b % 2], 16)
                act.preload_act_table_set("natural_log_exp_and_others")
                act.wait_ge(o_all, 1)
                act.wait_ge(new_out[0], 16 * 4)
                act.wait_ge(new_out[1], 16 * 4)
                for h in range(H):
                    if h:
                        act.wait_ge(osum, h)
                    act.activation(osq[:, :], q_[:, h, :], ACT.Square).then_inc(osq_made, 1)
                    act.wait_ge(osum, h + 1)
                    if h:
                        act.wait_ge(y_step, 3 * h - 2)
                    o3 = orr[:, :].rearrange("p (c n) -> p c n", c=NC)
                    act.activation(o3, pm[:, 3:6, 0:CH], ACT.Ln, scale=1.0 / P, bias=eps[:, 0:1]).then_inc(orr_made, 1)
                    act.wait_ge(orr_made, 2 * h + 1)
                    act.activation(o3, o3, ACT.Exp, scale=-0.5).then_inc(orr_made, 1)
                for g in range(H):
                    for c in range(NC):
                        e = 3 * g + c
                        act.wait_ge(mixed, e + 1)
                        act.wait_ge(ya_made, g + 1)
                        act.activation(y_hi[:, 4 + g, c * CH:(c + 1) * CH], bank[3 + e % 3][:, 0:CH], ACT.Copy,
                                       scale=pscale[:, g:g + 1]).then_inc(yb_hi, 1)

            def norm_factors(n):
                act.preload_act_table_set("natural_log_exp_and_others")
                act.wait_ge(sq_wide, n)
                r3_ = rb[:, :].rearrange("p (c n) -> p c n", c=NC)
                act.wait_ge(evac, ph["cq"].done if n == 1 else ph["in0"].done)
                act.activation(r3_, pm[:, 3:6, 0:CH], ACT.Ln, scale=1.0 / D, bias=eps[:, 0:1]).then_inc(rb_made, 1)
                act.wait_ge(rb_made, 2 * n)
                act.activation(r3_, r3_, ACT.Exp, scale=-0.5).then_inc(rb_made, 1)

            def split_only(p):
                def body(i, last):
                    for s in range(2):
                        split_next(p, i, s, last)
                pairs(act, p, body)

            def memory_in():
                for n in range(2):
                    act.wait_ge(mem_in, 32)
                    if n:
                        act.wait_ge(mem_sq, n)
                    act.activation(mjunk[:, :], mtok[:, n, :], ACT.Square,
                                   accum_out=ss[:, 9 + n:10 + n]).then_inc(mem_sq, 1)
                act.wait_ge(mem_sq, 2)
                act.activation(rtok[:, 9:11], ss[:, 9:11], ACT.Ln, scale=1.0 / D, bias=eps[:, 0:1]).then_inc(mem_sq, 1)
                act.wait_ge(mem_sq, 3)
                act.activation(rtok[:, 9:11], rtok[:, 9:11], ACT.Exp, scale=-0.5).then_inc(mem_sq, 1)

            def q_block(n):
                if not isinstance(n, int) or n:
                    act.wait_ge(sc_done, n)
                act.wait_ge(evac, ph["kv"].done)
                act.activation(qs[:, :, :], qT[:, :, bass.ds(n * P, P)], ACT.Copy).then_inc(qs_made, 1)

            def exps(n):
                act.wait_ge(mx_made, n + 1)
                if not isinstance(n, int) or n:
                    act.wait_ge(pt_done, n)
                for h in range(H):
                    last = act.activation(pr[:, h, :], wide(0)[:, h * XD:(h + 1) * XD], ACT.Exp, scale=SCALE,
                                          bias=nmax[:, h:h + 1], accum_out=den[:, h:h + 1])
                last.then_inc(ex_made, 1)

            def attention():
                q_block(0)
                exps(0)

                def body(n, more):
                    if more:
                        q_block(n + 1)
                    act.wait_ge(pt_done, n + 1)
                    act.wait_ge(pv_done, n + 1)
                    act.activation(prT[:, :, :], wide(2).rearrange("p (k c) -> p k c", k=KB), ACT.Copy).then_inc(pt_out, 1)
                    if more:
                        exps(n + 1)
                with act.Fori(0, PAIRS - 1) as n:
                    body(n, True)
                body(PAIRS - 1, False)

            def sample_softmax():
                act.wait_ge(ssm, 2)
                act.activation(sp_[:, :, :], bank[4][0:32, 0:M].rearrange("p (a c) -> p a c", a=2), ACT.Exp, scale=SCALE,
                               bias=sst[:, 1:2], accum_out=sst[:, 2:3]).then_inc(sex, 1)

            for p in live[2:]:
                if p.name == "out":
                    mixer_end()
                    split_only(p)
                    norm_factors(1)
                elif p.name == "cq":
                    split_only(p)
                    memory_in()
                elif p.name == "kv":
                    split_only(p)
                    attention()
                    sample_softmax()
                elif p.name == "co":
                    split_only(p)
                    norm_factors(2)
                elif p.name.startswith("in"):
                    g0 = int(p.name[2:])

                    def body(i, last):
                        split_next(p, i, 0, last)
                        for c in range(NC):
                            act.wait_ge(evac, p.done + 6 * i + c + 1)
                            cc = fa[:, c * CH:(c + 1) * CH]
                            act.activation(cc, cc, ACT.Silu).then_inc(silu_made, 1)
                            if c == 1:
                                split_next(p, i, 1, last)
                    pairs(act, p, body)
                else:
                    split_only(p)
            if stop is None:
                for n in range(9):
                    rows = P if n < 8 else NS
                    act.wait_ge(y_turned, n + 1)
                    if n:
                        act.wait_ge(yfac, 3 * n)
                    act.activation(yjunk[0:rows, :], wide(3 + 2 * (n % 2))[0:rows, :], ACT.Square,
                                   accum_out=ss[0:rows, n:n + 1]).then_inc(yfac, 1)
                    act.wait_ge(yfac, 3 * n + 1)
                    act.activation(fac[0:rows, n:n + 1], ss[0:rows, n:n + 1], ACT.Ln, scale=1.0 / D,
                                   bias=eps[0:rows, 0:1]).then_inc(yfac, 1)
                    act.wait_ge(yfac, 3 * n + 2)
                    act.activation(fac[0:rows, n:n + 1], fac[0:rows, n:n + 1], ACT.Exp, scale=-0.5).then_inc(yfac, 1)

        @block.vector
        def _(dve):
            dve.memset(ss[:, :], 1.0).then_inc(chain, 1)
            dve.memset(fac[:, 1:16], 0.0).then_inc(evac, 4)
            dve.memset(rtok[:, :], 0.0).then_inc(o_out, 1)
            dve.memset(fac[:, 0:1], 0.0).then_inc(pv_out, 1)
            dve.wait_ge(const_in, 16 * 6)
            dve.tensor_tensor(lbw[:, 2, :], lbt[:, 0, :], lbt[:, 1, :], ALU.max).then_inc(chain, 1)
            dve.wait_ge(chain, 2)
            dve.tensor_tensor(lbt[:, :, :], lbt[:, :, :], lbw[:, 2:3, :].to_broadcast([P, 2, H]),
                              ALU.subtract).then_inc(chain, 1)

            def split_lo(n_):
                p, i, s = n_
                dve.wait_ge(hi_made, p.first + 2 * i + s + 1)
                dve.tensor_tensor(w_lo[s][:, :, :], raw[:, s, :, :], w_hi[s][:, :, :].bitcast(F32),
                                  ALU.subtract).then_inc(lo_made, 1)

            split_lo((phases[0], 0, 0))
            for n in range(9):
                cols = P if n < 8 else NS
                dve.wait_ge(x_turned, n + 1)
                src = wide(3 + 2 * (n % 2)).rearrange("p (k c) -> p k c", k=KB)[:, :, 0:cols]
                h_, l_ = x_hi[:, :, n * P:n * P + cols], x_lo[:, :, n * P:n * P + cols]
                dve.tensor_copy(h_, src).then_inc(x_split, 1)
                dve.wait_ge(x_split, 2 * n + 1)
                dve.tensor_tensor(l_, src, h_.bitcast(F32), ALU.subtract).then_inc(x_split, 1)
            dve.wait_ge(r_made, 2)
            dve.tensor_tensor(lbw[:, 2, :], lbw[:, 0, :], lbw[:, 1, :], ALU.add).then_inc(chain, 1)
            dve.wait_ge(chain, 4)
            dve.reciprocal(lbw[:, 3, :], lbw[:, 2, :]).then_inc(chain, 1)
            dve.wait_ge(chain, 5)
            dve.tensor_tensor(omlb[:, :], lbw[:, 1, :], lbw[:, 3, :], ALU.mult).then_inc(chain, 1)
            dve.wait_ge(r_wide, 1)
            dve.tensor_copy(rb[:, :], wide(5, 3)[:, 0:T]).then_inc(rb_made, 1)
            dve.wait_ge(rb_made, 1)

            def plain_evac(p, i, s, c, dst):
                dve.wait_ge(mm_done, p.done + 6 * i + 3 * s + c + 1)
                dve.tensor_tensor(dst, bank[c][:, 0:CH], rb[:, c * CH:(c + 1) * CH], ALU.mult).then_inc(evac, 1)

            def qfi_body(i, last):
                p = ph["qfi"]
                for s in range(2):
                    for c in range(NC):
                        plain_evac(p, i, s, c, proj[:, bass.ds(2 * i + s, 1), c * CH:(c + 1) * CH].squeeze(1))
                        if c == 0:
                            n = nxt(p, i, s, last)
                            if n:
                                split_lo(n)
            pairs(dve, ph["qfi"], qfi_body)

            def flat(x):
                return x[:, :, :].rearrange("p h c -> p (h c)")

            def decays(i, s):
                n = 2 * i + s
                dve.wait_ge(lf_made, n + 1)
                dve.tensor_tensor_scan(flat(hg["b"]), keep[:, :], flat(hg["lf"]), 0.0, ALU.mult,
                                       ALU.add).then_inc(b_made, 1)
                dve.wait_ge(b_made, n + 1)
                b4 = flat(hg["b"]).rearrange("p (n c) -> p n c", c=C)
                dve.tensor_tensor(flat(hg["lf"]).rearrange("p (n c) -> p n c", c=C),
                                  b4[:, :, C - 1:C].to_broadcast([P, 8, C]), b4, ALU.subtract).then_inc(e_made, 1)
                dve.tensor_tensor(flat(hg["d"]).rearrange("p (n c) -> p n c", c=C), b4,
                                  b4[:, :, MID:MID + 1].to_broadcast([P, 8, C]), ALU.subtract).then_inc(d_made, 1)

            def weigh(i, s):
                n = 2 * i + s
                qv, kv = q_[:, :, bass.ds(n * P, P)], f_[:, :, bass.ds(n * P, P)]
                e3 = hg["e3a" if s == 0 else "e3b"]
                dve.wait_ge(exp_e, n + 1)
                dve.tensor_tensor(hg["e4"][:, :, :], hg["e4"][:, :, :], kv, ALU.mult).then_inc(kn_made, 1)
                dve.wait_ge(exp_b, n + 1)
                dve.tensor_tensor(e3[:, :, :], e3[:, :, :], qv, ALU.mult).then_inc(qb_made, 1)
                dve.wait_ge(exp_d, n + 1)
                dve.tensor_tensor(hg["e1"][:, :, :], hg["e1"][:, :, :], qv, ALU.mult)
                dve.tensor_tensor(hg["e2"][:, :, :], hg["e2"][:, :, :], kv, ALU.mult).then_inc(qk_made, 1)

            def mask(i, s):
                dve.copy_predicated(hg["am"][:, :, :], cmask[:, :].unsqueeze(1).to_broadcast([P, H, P]),
                                    bank[5].rearrange("p (h c) -> p h c", h=H)).then_inc(masked, 1)

            def state(i, s, x):
                a, b_ = (hg["S0"], hg["S1"]) if x == 0 else (hg["S1"], hg["S0"])
                n = 2 * i + s
                if x == 0:
                    dve.wait_ge(ap_done, n + 2)
                    dve.wait_ge(o_done, n + 2)
                    dve.wait_ge(S0_made, n + 1)
                else:
                    dve.wait_ge(S1_made, n + 1)
                for h in range(H):
                    last = dve.scalar_tensor_tensor(b_[:, h, :], a[:, h, :], ebs[:, s, h, x:x + 1],
                                                    bank[6 + x][:, h * P:(h + 1) * P], ALU.mult, ALU.add)
                last.then_inc(S1_made if x == 0 else S0_made, 1)

            def outputs(i, s):
                n = 2 * i + s
                dve.wait_ge(o_done, n + 3)
                dve.tensor_scalar(q_[:, :, bass.ds(n * P, P)], bank[3].rearrange("p (h c) -> p h c", h=H), 1.0, None,
                                  ALU.mult).then_inc(o_out, 1)

            dve.memset(hg["am"][:, :, :], 0.0).then_inc(masked, 1)
            dve.memset(hg["S0"][:, :, :], 0.0).then_inc(S0_made, 1)
            dve.wait_ge(q_act, 1)
            dve.wait_ge(masked, 1)
            decays(0, 0)
            weigh(0, 0)
            p = ph["gu"]

            def gu_body(i, last):
                for s in range(2):
                    n = nxt(p, i, s, last)
                    dst = proj[:, bass.ds(12 + 2 * i + s, 1), :].squeeze(1)
                    more = n and n[0] is p
                    plain_evac(p, i, s, 0, dst[:, 0:CH])
                    if n:
                        split_lo(n)
                    if more:
                        decays(n[1], n[2])
                    plain_evac(p, i, s, 1, dst[:, CH:2 * CH])
                    state(i, s, 0)
                    mask(i, s)
                    plain_evac(p, i, s, 2, dst[:, 2 * CH:T])
                    outputs(i, s)
                    state(i, s, 1)
                    if more:
                        weigh(n[1], n[2])
            if p in live:
                pairs(dve, p, gu_body)

            def mixer_end():
                dve.wait_ge(o_done, PAIRS + 2)
                dve.tensor_scalar(fs[:, :, :], f_[:, :, TP:T], -1.0, 1.0, ALU.mult, ALU.add).then_inc(fs_made, 1)
                dve.wait_ge(fs_made, 1)
                for b in range(NS):
                    so, sn, at_b = s_old[b % 2], s_new[b % 2], slice(TP + b, TP + b + 1)
                    dve.wait_ge(old_in[b % 2], 16 * (b // 2 + 1))
                    dve.tensor_tensor(so[:, :, :], so[:, :, :], fs[:, :, b:b + 1].to_broadcast([P, H, P]),
                                      ALU.mult).then_inc(fs_made, 1)
                    dve.wait_ge(v_wide, b + 1)
                    if b >= 2:
                        dve.wait_ge(new_out[b % 2], 16 * (b // 2))
                        dve.wait_ge(new_read, b - 1)
                    dve.tensor_tensor(sn[:, :, :], bank[6 + b % 2].rearrange("p (h v) -> p h v", h=H),
                                      f_[:, :, at_b].to_broadcast([P, H, P]), ALU.mult).then_inc(new_made, 1)
                    dve.wait_ge(fs_made, b + 2)
                    dve.wait_ge(new_made, 2 * b + 1)
                    dve.tensor_tensor(sn[:, :, :], sn[:, :, :], so[:, :, :], ALU.add).then_inc(new_made, 1)
                dve.wait_ge(past_made, 1)
                dve.wait_ge(u_turned, 1)
                for g, w in enumerate(POOLW):
                    us = u_[:, g, TP:T]
                    rows = pastT[:, g, :].rearrange("p (b r) -> p b r", b=NS)[:, :, PAST - (w - 1):PAST]
                    dve.tensor_reduce(psums[:, g, :], rows, AX_X, ALU.add).then_inc(spooled, 1)
                    dve.wait_ge(spooled, 3 * g + 1)
                    dve.tensor_tensor(psums[:, g, :], psums[:, g, :], us, ALU.add).then_inc(spooled, 1)
                    dve.wait_ge(spooled, 3 * g + 2)
                    dve.scalar_tensor_tensor(us, psums[:, g, :], 1.0 / w, us, ALU.mult, ALU.subtract).then_inc(spooled, 1)
                dve.wait_ge(new_read, NS)
                dve.tensor_copy(q_[:, :, TP:T], bank[4][:, 0:H * NS].rearrange("p (h b) -> p h b", h=H)).then_inc(o_all, 1)
                dve.wait_ge(o_all, 1)
                dve.wait_ge(g_act, 1)
                for h in range(H):
                    o = q_[:, h, :]
                    dve.wait_ge(orr_made, 2 * h + 2)
                    dve.scalar_tensor_tensor(o, o, hnorm[:, h:h + 1], orr[:, :], ALU.mult, ALU.mult).then_inc(y_step, 1)
                    dve.wait_ge(y_step, 3 * h + 1)
                    dve.tensor_tensor(o, o, g_[:, h, :], ALU.mult).then_inc(y_step, 1)
                    dve.wait_ge(y_step, 3 * h + 2)
                    dve.tensor_copy(y_hi[:, h, :], o).then_inc(y_step, 1)
                    dve.wait_ge(y_step, 3 * h + 3)
                    dve.tensor_tensor(y_lo[:, h, :], o, y_hi[:, h, :].bitcast(F32), ALU.subtract).then_inc(ya_made, 1)
                for g in range(H):
                    for c in range(NC):
                        e = 3 * g + c
                        dve.wait_ge(yb_hi, e + 1)
                        dve.scalar_tensor_tensor(y_lo[:, 4 + g, c * CH:(c + 1) * CH], bank[3 + e % 3][:, 0:CH],
                                                 pscale[:, g:g + 1], y_hi[:, 4 + g, c * CH:(c + 1) * CH].bitcast(F32),
                                                 ALU.mult, ALU.subtract).then_inc(yb_made, 1)

            def residual(p):
                at = 0 if p.name == "out" else 8 * NC

                def body(i, last):
                    for s in range(2):
                        for c in range(NC):
                            e = 6 * i + 3 * s + c
                            xn = xnew[:, (3 * s + c) % 2, :]
                            xh = x_hi[:, bass.ds(2 * i + s, 1), c * CH:(c + 1) * CH].squeeze(1)
                            xl = x_lo[:, bass.ds(2 * i + s, 1), c * CH:(c + 1) * CH].squeeze(1)
                            dve.wait_ge(sq_made, at + e + 1)
                            dve.wait_ge(mm_done, p.done + e + 1)
                            dve.tensor_tensor(xn, bank[c][:, 0:CH], xh.bitcast(F32), ALU.add).then_inc(evac, 1)
                            dve.wait_ge(evac, p.done + e + 1)
                            dve.tensor_tensor(xn, xn, xl.bitcast(F32), ALU.add).then_inc(xsum, 1)
                            dve.wait_ge(xsum, at + e + 1)
                            dve.tensor_scalar(xh, xn, 1.0, None, ALU.mult).then_inc(xh_made, 1)
                            dve.wait_ge(xh_made, at + e + 1)
                            dve.tensor_tensor(xl, xn, xh.bitcast(F32), ALU.subtract).then_inc(xl_made, 1)
                            if c == 0:
                                n = nxt(p, i, s, last)
                                if n:
                                    split_lo(n)
                pairs(dve, p, body)

            def queries(p):
                dve.wait_ge(rb_made, 3)

                def body(i, last):
                    for s in range(2):
                        for c in range(NC):
                            plain_evac(p, i, s, c, qT[:, bass.ds(2 * i + s, 1), c * CH:(c + 1) * CH].squeeze(1))
                            if c == 0:
                                n = nxt(p, i, s, last)
                                if n:
                                    split_lo(n)
                pairs(dve, p, body)
                for n in range(2):
                    dve.wait_ge(mem_turned, n + 1)
                    if n:
                        dve.wait_ge(mem_step, 3)
                    dve.tensor_tensor(mf[:, :, :], wide(3 + 2 * n).rearrange("p (k c) -> p k c", k=KB),
                                      gmem[:, :].unsqueeze(2).to_broadcast([P, KB, P]), ALU.mult).then_inc(mem_step, 1)
                    dve.wait_ge(mem_step, 3 * n + 1)
                    mh, ml = m_hi[:, :, n * P:(n + 1) * P], m_lo[:, :, n * P:(n + 1) * P]
                    dve.tensor_copy(mh, mf[:, :, :]).then_inc(mem_step, 1)
                    dve.wait_ge(mem_step, 3 * n + 2)
                    dve.tensor_tensor(ml, mf[:, :, :], mh.bitcast(F32), ALU.subtract).then_inc(mem_step, 1)
                dve.wait_ge(rbm_wide, 1)
                dve.tensor_copy(rbm[:, :], bank[7][:, 0:M]).then_inc(rbm_made, 1)
                dve.wait_ge(rbm_made, 1)

            def keys_values(p):
                def body(i, last):
                    for s in range(2):
                        n = nxt(p, i, s, last)
                        if n:
                            split_lo(n)
                        dve.wait_ge(mm_done, p.done + 2 * i + s + 1)
                        dve.tensor_tensor(kvT[:, bass.ds(2 * i + s, 1), :].squeeze(1), bank[s][:, 0:M], rbm[:, :],
                                          ALU.mult).then_inc(evac, 1)
                pairs(dve, p, body)
                for x in range(4):
                    dve.wait_ge(kv_turned, x + 1)
                    dve.tensor_copy((knat, vnat)[x // 2][:, x % 2, :], wide(3 + 2 * (x % 2))).then_inc(kv_nat, 1)

            def attention():
                def maxima(n):
                    dve.wait_ge(sc_done, n + 1)
                    dve.tensor_reduce(smax[:, :], wide(0).rearrange("p (h m) -> p h m", h=H), AX_X,
                                      ALU.max).then_inc(mx_step, 1)
                    dve.wait_ge(mx_step, n + 1)
                    dve.tensor_scalar(nmax[:, :], smax[:, :], -SCALE, None, ALU.mult).then_inc(mx_made, 1)

                def normalize(n):
                    dve.wait_ge(ex_made, n + 1)
                    dve.reciprocal(rden[:, :], den[:, :]).then_inc(rd_made, 1)
                    dve.wait_ge(rd_made, n + 1)
                    dve.tensor_tensor(pr[:, :, :], pr[:, :, :], rden[:, :].unsqueeze(2).to_broadcast([P, H, XD]),
                                      ALU.mult).then_inc(p_made, 1)

                def outputs_(n):
                    dve.wait_ge(pv_done, n + 2)
                    src = wide(4).rearrange("p (k c) -> p k c", k=KB)
                    oh = o_hi[:, :, bass.ds(n * P, P)]
                    dve.tensor_scalar(oh, src, 1.0, None, ALU.mult).then_inc(pv_hi, 1)
                    dve.wait_ge(pv_hi, n + 1)
                    dve.tensor_tensor(o_lo[:, :, bass.ds(n * P, P)], src, oh.bitcast(F32), ALU.subtract).then_inc(pv_out, 1)

                maxima(0)
                normalize(0)
                dve.wait_ge(kn_out, 16)
                with dve.Fori(0, PAIRS - 1) as n:
                    maxima(n + 1)
                    normalize(n + 1)
                    outputs_(n)
                outputs_(PAIRS - 1)
                dve.wait_ge(pv_out, PAIRS + 1)
                for b in range(NS):
                    dve.wait_ge(kc_in[b % 2], 16 * (b // 2 + 1))
                    dve.wait_ge(sq_w, b + 1)
                    for a in range(2):
                        for h in range(H):
                            kk = kc[b % 2][:, a, h * XD:(h + 1) * XD]
                            last = dve.tensor_tensor_reduce(kk, kk, wide(2 * (b % 2))[:, h * XD:(h + 1) * XD], 1.0, 0.0,
                                                            ALU.mult, ALU.add, ssc[:, a, b * H + h:b * H + h + 1])
                    last.then_inc(ssc_made, 1)
                dve.wait_ge(ssc_turned, 1)
                dve.tensor_reduce(sst[:, 0:1], bank[4][0:32, 0:M], AX_X, ALU.max).then_inc(ssm, 1)
                dve.wait_ge(ssm, 1)
                dve.tensor_scalar(sst[:, 1:2], sst[:, 0:1], -SCALE, None, ALU.mult).then_inc(ssm, 1)
                dve.wait_ge(sex, 1)
                dve.reciprocal(sst[:, 3:4], sst[:, 2:3]).then_inc(ssm, 1)
                dve.wait_ge(ssm, 3)
                dve.tensor_scalar(sp_[:, :, :], sp_[:, :, :], sst[:, 3:4], None, ALU.mult).then_inc(ssm, 1)
                dve.wait_ge(sp_turned, 1)
                dve.tensor_copy(spT[:, :, :], bank[5][:, 0:64].rearrange("p (a b) -> p a b", a=2)).then_inc(ssm, 1)
                dve.wait_ge(sv_done, NS)
                src = bank[6][:, 0:64].rearrange("p (k b) -> p k b", k=KB)
                dve.tensor_copy(o_hi[:, :, TP:T], src).then_inc(so_made, 1)
                dve.wait_ge(so_made, 1)
                dve.tensor_tensor(o_lo[:, :, TP:T], src, o_hi[:, :, TP:T].bitcast(F32), ALU.subtract).then_inc(so_made, 1)

            def ffn_in(p):
                f0 = int(p.name[2:])

                def body(i, last):
                    for c in range(NC):
                        plain_evac(p, i, 0, c, fa[:, c * CH:(c + 1) * CH])
                        if c == 0:
                            split_lo(nxt(p, i, 0, last))
                    for c in range(NC):
                        plain_evac(p, i, 1, c, fp[:, c % 2, :])
                        n = 3 * (f0 + i) + c + 1
                        dve.wait_ge(evac, p.done + 6 * i + 3 + c + 1)
                        dve.wait_ge(silu_made, n)
                        dve.tensor_tensor(fp[:, c % 2, :], fp[:, c % 2, :], fa[:, c * CH:(c + 1) * CH],
                                          ALU.mult).then_inc(fprod, 1)
                        sh = s_hi[:, bass.ds(i, 1), c * CH:(c + 1) * CH].squeeze(1)
                        sl = s_lo[:, bass.ds(i, 1), c * CH:(c + 1) * CH].squeeze(1)
                        dve.wait_ge(fprod, n)
                        dve.tensor_scalar(sh, fp[:, c % 2, :], 1.0, None, ALU.mult).then_inc(s_hi_made, 1)
                        dve.wait_ge(s_hi_made, n)
                        dve.tensor_tensor(sl, fp[:, c % 2, :], sh.bitcast(F32), ALU.subtract).then_inc(s_made, 1)
                        if c == 0:
                            split_lo(nxt(p, i, 1, last))
                pairs(dve, p, body)

            def ffn_down(p):
                first = p.name == "down0"
                if not first:
                    dve.wait_ge(acc_made, 8 * NC)
                    dve.wait_ge(evac, p.done)

                def body(i, last):
                    for s in range(2):
                        for c in range(NC):
                            e = 6 * i + 3 * s + c
                            at_ = (bass.ds(2 * i + s, 1), slice(c * CH, (c + 1) * CH))
                            a = acc[:, at_[0], at_[1]].squeeze(1)
                            dve.wait_ge(mm_done, p.done + e + 1)
                            add = x_hi[:, at_[0], at_[1]].squeeze(1).bitcast(F32) if first else a
                            dve.tensor_tensor(a, bank[c][:, 0:CH], add, ALU.add).then_inc(evac, 1)
                            if first:
                                dve.wait_ge(evac, p.done + e + 1)
                                dve.tensor_tensor(a, a, x_lo[:, at_[0], at_[1]].squeeze(1).bitcast(F32),
                                                  ALU.add).then_inc(acc_made, 1)
                            if c == 0:
                                n = nxt(p, i, s, last)
                                if n:
                                    split_lo(n)
                pairs(dve, p, body)

            for p in live[2:]:
                if p.name == "out":
                    mixer_end()
                    residual(p)
                elif p.name == "cq":
                    queries(p)
                elif p.name == "kv":
                    keys_values(p)
                    attention()
                elif p.name == "co":
                    residual(p)
                    dve.wait_ge(rb_made, 5)
                elif p.name.startswith("in"):
                    ffn_in(p)
                else:
                    ffn_down(p)
            if stop is None:
                dve.wait_ge(gfin_in, 16)
                for n in range(9):
                    rows = P if n < 8 else NS
                    dve.wait_ge(yfac, 3 * n + 3)
                    if n >= 2:
                        dve.wait_ge(y_out[n % 2], 16 * (n // 2))
                    dve.scalar_tensor_tensor(ytok[n % 2][0:rows, :], wide(3 + 2 * (n % 2))[0:rows, :],
                                             fac[0:rows, n:n + 1], gfin[0:rows, :], ALU.mult, ALU.mult).then_inc(y_made, 1)

        @block.tensor
        def _(pe):
            def stripe_chunk(p, i, s, c, hi, lo, kb=KB, cols=CH, out=None):
                out = bank[c][:, 0:cols] if out is None else out
                x0 = c * CH
                for k in range(kb):
                    pe.matmul(out, w_hi[s][:, k, :], hi[:, k, x0:x0 + cols], start=(k == 0), stop=False)
                    pe.matmul(out, w_hi[s][:, k, :], lo[:, k, x0:x0 + cols], start=False, stop=False)
                    last = pe.matmul(out, w_lo[s][:, k, :], hi[:, k, x0:x0 + cols], start=False, stop=(k == kb - 1))
                last.then_inc(mm_done, 1)

            def chunk(p, i, s, c, hi, lo, kb=KB):
                if c == 0:
                    pe.wait_ge(lo_made, p.first + 2 * i + s + 1)
                pe.wait_ge(evac, p.done + 6 * i + 3 * s - 2 + c)
                stripe_chunk(p, i, s, c, hi, lo, kb)

            pe.wait_ge(setup, 10)
            for n in range(9):
                rows = P if n < 8 else NS
                pe.wait_ge(x_in[n], 16)
                if n >= 2:
                    pe.wait_ge(x_split, 2 * (n - 1))
                for k in range(KB):
                    last = pe.transpose(wide(3 + 2 * (n % 2))[:, k * P:k * P + rows],
                                        xt[n][0:rows, k * P:(k + 1) * P], ident[0:rows, 0:rows])
                    if n == 0 and k < 5:
                        last.then_inc((mm_done, turned, ap_done, o_done, pv_done)[k], (4, 1, 1, 2, 1)[k])
                last.then_inc(x_turned, 1)
            pe.wait_ge(x_split, 18)
            pe.wait_ge(r_made, 1)
            for n in range(9):
                cols = P if n < 8 else NS
                last = pe.matmul(wide(5, 3)[:, n * P:n * P + cols], rtok[:, n:n + 1].to_broadcast([P, P]),
                                 ident[:, 0:cols], start=True, stop=True)
            last.then_inc(r_wide, 1)

            with pe.Fori(0, 6) as i:
                for s in range(2):
                    for c in range(NC):
                        chunk(ph["qfi"], i, s, c, x_hi, x_lo)

            def turn(i, s):
                n = 2 * i + s
                pe.wait_ge(kn_made, n + 1)
                pe.wait_ge(iv_made, n + 1)
                pe.wait_ge(o_out, n + 1)
                for h in range(H):
                    pe.transpose(bank[3][:, h * P:(h + 1) * P], hg["e4"][:, h, :], ident[:, :])
                for h in range(H):
                    last = pe.transpose(bank[4][:, h * P:(h + 1) * P], hg["iv"][:, h, :], ident[:, :])
                last.then_inc(turned, 1)

            def scores(i, s):
                n = 2 * i + s
                pe.wait_ge(qk_made, n + 1)
                pe.wait_ge(kv_out, n + 1)
                pe.wait_ge(masked, n + 1)
                pe.wait_ge(S0_made, n + 1)
                for h in range(H):
                    pe.matmul(bank[5][:, h * P:(h + 1) * P], hg["e2"][:, h, :], hg["e1"][:, h, :], start=True, stop=True)
                for x in range(2):
                    for h in range(H):
                        last = pe.matmul(bank[6 + x][:, h * P:(h + 1) * P], hg["kt"][x * C:(x + 1) * C, h, :],
                                         hg["vt"][x * C:(x + 1) * C, h, :], start=True, stop=True)
                last.then_inc(ap_done, 1)

            def reads(i, s):
                n = 2 * i + s
                e3 = hg["e3a" if s == 0 else "e3b"]
                pe.wait_ge(masked, n + 2)
                pe.wait_ge(qb_made, n + 1)
                pe.wait_ge(S1_made, n + 1)
                for h in range(H):
                    o = bank[3][:, h * P:(h + 1) * P]
                    pe.matmul(o, hg["vt"][:, h, :], hg["am"][:, h, :], start=True, stop=False)
                    pe.matmul(o[:, 0:C], hg["S0"][:, h, :], e3[:, h, 0:C], start=False, stop=False)
                    last = pe.matmul(o[:, C:P], hg["S1"][:, h, :], e3[:, h, C:P], start=False, stop=True)
                last.then_inc(o_done, 1)

            if ph["gu"] in live:
                with pe.Fori(0, 4) as i:
                    for s in range(2):
                        chunk(ph["gu"], i, s, 0, x_hi, x_lo)
                        turn(i, s)
                        chunk(ph["gu"], i, s, 1, x_hi, x_lo)
                        scores(i, s)
                        chunk(ph["gu"], i, s, 2, x_hi, x_lo)
                        reads(i, s)

            def mixer_end():
                pe.wait_ge(evac, ph["gu"].done + 8 * NC)
                pe.wait_ge(o_out, PAIRS + 1)
                for g in range(H):
                    last = pe.transpose(bank[3][0:23, g * P:(g + 1) * P], u_[:, g, TP - PAST:T], ident[:, :])
                last.then_inc(u_turned, 1)
                pe.wait_ge(past_in, 16)
                pe.wait_ge(masked, PAIRS + 1)
                for g in range(H):
                    last = pe.transpose(bank[5][:, g * 120:(g + 1) * 120], past[0:120, g * P:(g + 1) * P],
                                        ident[0:120, 0:120])
                last.then_inc(past_turned, 1)
                pe.wait_ge(S0_made, PAIRS + 1)

                def spread_v(b):
                    if b >= 2:
                        pe.wait_ge(new_made, 2 * (b - 2) + 1)
                    for h in range(H):
                        last = pe.matmul(bank[6 + b % 2][:, h * P:(h + 1) * P],
                                         i_[:, h, TP + b:TP + b + 1].to_broadcast([P, P]), ident[:, :],
                                         start=True, stop=True)
                    last.then_inc(v_wide, 1)

                spread_v(0)
                for b in range(NS):
                    if b + 1 < NS:
                        spread_v(b + 1)
                    pe.wait_ge(new_made, 2 * b + 2)
                    for h in range(H):
                        last = pe.matmul(bank[4][:, h * NS + b:h * NS + b + 1], s_new[b % 2][:, h, :],
                                         q_[:, h, TP + b:TP + b + 1], start=True, stop=True)
                    last.then_inc(new_read, 1)
                for h in range(H):
                    pe.wait_ge(osq_made, h + 1)
                    if h:
                        pe.wait_ge(orr_made, 2 * h)
                    for c in range(NC):
                        last = pe.matmul(bank[3 + c][:, 0:CH], ones[:, :], osq[:, c * CH:(c + 1) * CH],
                                         start=True, stop=True)
                    last.then_inc(osum, 1)
                pe.wait_ge(orr_made, 2 * H)
                pe.wait_ge(misc_in, 16)
                pe.wait_ge(spooled, 3 * H)
                for g in range(H):
                    pe.wait_ge(pooled, g + 1)
                    for c in range(NC):
                        e = 3 * g + c
                        if e >= 3:
                            pe.wait_ge(yb_made, e - 2)
                        pe.matmul(bank[3 + e % 3][:, 0:CH], pmix[:, g, :], u_[:, g, c * CH:(c + 1) * CH],
                                  start=True, stop=True).then_inc(mixed, 1)
                pe.wait_ge(ya_made, H)
                pe.wait_ge(yb_made, 3 * H)

            def norm_sums(n):
                pe.wait_ge(sq_added, 8 * NC * n)
                for c in range(NC):
                    last = pe.matmul(bank[3 + c][:, 0:CH], ones[:, :], sqacc[:, c * CH:(c + 1) * CH], start=True, stop=True)
                last.then_inc(sq_wide, 1)
                pe.wait_ge(xl_made, 8 * NC * n)

            def product(p, hi, lo, kb=KB):
                with pe.Fori(0, p.stripes // 2) as i:
                    for s in range(2):
                        for c in range(NC):
                            chunk(p, i, s, c, hi, lo, kb)

            def memory_in():
                pe.wait_ge(mem_in, 32)
                pe.wait_ge(rb_made, 3)
                for n in range(2):
                    for k in range(KB):
                        last = pe.transpose(wide(3 + 2 * n)[:, k * P:(k + 1) * P], mtok[:, n, k * P:(k + 1) * P], ident[:, :])
                    last.then_inc(mem_turned, 1)
                pe.wait_ge(mem_sq, 4)
                for n in range(2):
                    last = pe.matmul(bank[7][:, n * P:(n + 1) * P], rtok[:, 9 + n:10 + n].to_broadcast([P, P]),
                                     ident[:, :], start=True, stop=True)
                last.then_inc(rbm_wide, 1)
                pe.wait_ge(mem_step, 6)
                pe.wait_ge(evac, ph["kv"].done)

            def keys_values(p):
                with pe.Fori(0, p.stripes // 2) as i:
                    for s in range(2):
                        pe.wait_ge(lo_made, p.first + 2 * i + s + 1)
                        pe.wait_ge(evac, p.done + 2 * i + s - 1)
                        stripe_chunk(p, i, s, 0, m_hi, m_lo, cols=M, out=bank[s][:, 0:M])
                pe.wait_ge(evac, ph["co"].done)
                for x in range(4):
                    if x >= 2:
                        pe.wait_ge(kv_nat, x - 1)
                    for k in range(KB):
                        last = pe.transpose(wide(3 + 2 * (x % 2))[:, k * P:(k + 1) * P],
                                            kvT[:, 8 * (x // 2) + k, (x % 2) * P:(x % 2 + 1) * P], ident[:, :])
                    last.then_inc(kv_turned, 1)

            def attention():
                def scores_(n):
                    pe.wait_ge(qs_made, n + 1)
                    if not isinstance(n, int) or n:
                        pe.wait_ge(ex_made, n)
                    for h in range(H):
                        for d in range(2):
                            last = pe.matmul(wide(0)[:, h * XD:(h + 1) * XD], qs[:, 2 * h + d, :], kvT[:, 2 * h + d, :],
                                             start=(d == 0), stop=(d == 1))
                    last.then_inc(sc_done, 1)

                def turn_p(n):
                    pe.wait_ge(p_made, n + 1)
                    for h in range(H):
                        for a in range(2):
                            last = pe.transpose(wide(2)[:, (2 * h + a) * P:(2 * h + a + 1) * P], pr[:, h, a * P:(a + 1) * P],
                                                ident[:, :])
                    last.then_inc(pt_done, 1)

                def values(n):
                    pe.wait_ge(pt_out, n + 1)
                    pe.wait_ge(pv_out, n + 1)
                    for h in range(H):
                        for d in range(2):
                            for a in range(2):
                                last = pe.matmul(wide(4)[:, (2 * h + d) * P:(2 * h + d + 1) * P],
                                                 vnat[:, a, h * XD + d * P:h * XD + (d + 1) * P], prT[:, 2 * h + a, :],
                                                 start=(a == 0), stop=(a == 1))
                    last.then_inc(pv_done, 1)

                scores_(0)
                pe.wait_ge(kv_nat, 4)
                with pe.Fori(0, PAIRS - 1) as n:
                    scores_(n + 1)
                    turn_p(n)
                    values(n)
                turn_p(PAIRS - 1)
                values(PAIRS - 1)

            def sample_attention():
                for b in range(NS):
                    pe.wait_ge(pt_out if b < 2 else ssc_made, PAIRS if b < 2 else b - 1)
                    for k in range(KB):
                        last = pe.matmul(wide(2 * (b % 2))[:, k * P:(k + 1) * P],
                                         qT[:, k, TP + b:TP + b + 1].to_broadcast([P, P]), ident[:, :],
                                         start=True, stop=True)
                    last.then_inc(sq_w, 1)
                pe.wait_ge(ssc_made, NS)
                pe.wait_ge(pv_out, PAIRS + 1)
                for a in range(2):
                    last = pe.transpose(bank[4][0:32, a * P:(a + 1) * P], ssc[:, a, :], ident[:, :])
                last.then_inc(ssc_turned, 1)
                pe.wait_ge(ssm, 4)
                for a in range(2):
                    last = pe.transpose(bank[5][:, a * 32:(a + 1) * 32], sp_[:, a, :], ident[0:32, 0:32])
                last.then_inc(sp_turned, 1)
                pe.wait_ge(ssm, 5)
                for b in range(NS):
                    pe.wait_ge(vc_in[b % 2], 16 * (b // 2 + 1))
                    for k in range(KB):
                        for a in range(2):
                            last = pe.matmul(bank[6][:, k * NS + b:k * NS + b + 1], vc[b % 2][:, a, k * P:(k + 1) * P],
                                             spT[:, a, b * H + k // 2:b * H + k // 2 + 1], start=(a == 0), stop=(a == 1))
                    last.then_inc(sv_done, 1)
                pe.wait_ge(so_made, 2)

            for p in live[2:]:
                if p.name == "out":
                    mixer_end()
                    product(p, y_hi, y_lo)
                elif p.name == "cq":
                    norm_sums(1)
                    product(p, x_hi, x_lo)
                elif p.name == "kv":
                    memory_in()
                    keys_values(p)
                    attention()
                    sample_attention()
                elif p.name == "co":
                    product(p, o_hi, o_lo)
                elif p.name.startswith("in"):
                    if p.name == "in0":
                        norm_sums(2)
                    product(p, x_hi, x_lo)
                else:
                    f0 = int(p.name[4:])
                    fb = dict(GROUPS)[f0]
                    pe.wait_ge(s_made, 3 * (f0 + fb))
                    product(p, s_hi, s_lo, fb)
            if stop is None:
                pe.wait_ge(evac, phases[-1].done + 8 * NC)
                for n in range(9):
                    rows = P if n < 8 else NS
                    if n >= 2:
                        pe.wait_ge(y_made, n - 1)
                    for k in range(KB):
                        last = pe.transpose(wide(3 + 2 * (n % 2))[0:rows, k * P:(k + 1) * P],
                                            acc[:, k, n * P:n * P + rows], ident[:, :])
                    last.then_inc(y_turned, 1)


INS = ["x_prompt", "x_sample", "mem_prompt", "state_hgrn", "state_pool", "cache_mem_k", "cache_mem_v", "g_mix",
       "w_in", "hgrn_lb", "hgrn_norm", "pool_mix", "pool_scale", "w_out", "g_mem", "w_mem_kv", "g_cross", "w_cq",
       "w_co", "g_ffn", "w_ffn_in", "w_ffn_out", "g_final"]
PER_LAYER = {"state_hgrn", "state_pool", "cache_mem_k", "cache_mem_v", "g_mix", "w_in", "hgrn_norm", "pool_mix",
             "pool_scale", "w_out", "g_mem", "w_mem_kv", "g_cross", "w_cq", "w_co", "g_ffn", "w_ffn_in", "w_ffn_out",
             "hgrn_prompt", "pool_prompt", "mem_k", "mem_v", "hgrn_sample", "pool_sample"}
OUTS = [("y_prompt", (1, TP, D)), ("y_sample", (NS, 1, D)), ("hgrn_prompt", (1, 1, H, P, P)),
        ("pool_prompt", (1, 1, PAST, W)), ("mem_k", (1, 1, M, H, XD)), ("mem_v", (1, 1, M, H, XD)),
        ("hgrn_sample", (1, NS, H, P, P)), ("pool_sample", (1, NS, PAST, W))]


def kernel(**inputs):
    import concourse.bacc as bacc
    from concourse.bass_utils import run_bass_kernel_spmd

    nc = bacc.Bacc("TRN2", target_bir_lowering=False, num_devices=1)
    arrays, t = {}, {}
    for name in INS:
        arrays["in_" + name] = a = np.ascontiguousarray(inputs[name])
        t[name] = nc.dram_tensor("in_" + name, a.shape, mybir.dt.from_np(a.dtype), kind="ExternalInput").ap()
    outs = OUTS if STOP is None else [("dbg", (20, P, T)), ("dbg2", (4, P, P))]
    for name, shape in outs:
        t[name] = nc.dram_tensor("out_" + name, shape, F32, kind="ExternalOutput").ap()
    hybrid_layer(nc, t, STOP)
    r = run_bass_kernel_spmd(nc, [arrays], core_ids=[0])
    return tuple(r.results[0]["out_" + name] for name, _ in outs)


STOP = None
```

```python
from contextlib import ExitStack

import numpy as np

import concourse.bass as bass
from concourse import mybir
from concourse.alu_op_type import AluOpType as ALU

ACT = mybir.ActivationFunctionType
F32 = mybir.dt.float32
F32R = mybir.dt.float32r
I32 = mybir.dt.int32
AX_X = mybir.AxisListType.X

P = 128
D = 1024
KB = D // P
TP = 1024
NS = 8
T = TP + NS
CH = 344
NC = T // CH
H = 4
W = 512
C = 64
MID = (C - 1) // 2
PAIRS = TP // (2 * C)
POOLW = (2, 4, 8, 16)
PAST = 15
M = 256
XD = 256
FF = 2816
FB = FF // P
GROUPS = ((0, 8), (8, 8), (16, 6))
EPS = 1e-6
LN_EXP = "natural_log_exp_and_others"
SCALE = XD ** -0.5
Y_BANKS = (3, 5, 0)


class Phase:

    def __init__(self, name, stripes, chunks, gain):
        self.name, self.stripes, self.chunks, self.gain = name, stripes, chunks, gain
        self.first = self.done = self.scaled = None


def make_phases():
    ph = [Phase("qfi", 12, NC, 0), Phase("gu", 8, NC, 0), Phase("out", 8, NC, None), Phase("cq", 8, NC, 1),
          Phase("kv", 16, 1, None), Phase("co", 8, NC, None)]
    for f0, fb in GROUPS:
        ph += [Phase(f"in{f0}", 2 * fb, NC, 2), Phase(f"down{f0}", 8, NC, None)]
    n, done, scaled = 0, 4, 0
    for p in ph:
        p.first, p.done, p.scaled = n, done, scaled
        n += p.stripes
        done += p.stripes * p.chunks
        scaled += p.stripes if p.gain is not None else 0
    return ph


def hybrid_layer(nc, t):
    t = {name: ap[0] if name in PER_LAYER else ap for name, ap in t.items()}
    phases = make_phases()
    ph = {p.name: p for p in phases}
    after = {a.name: b for a, b in zip(phases, phases[1:])}

    with ExitStack() as ctx:
        def sem(name):
            return ctx.enter_context(nc.semaphore(name))

        base = 16512
        spot = [base]

        def put(name, shape, dt=F32, at=None):
            free = int(np.prod(shape[1:])) * 4
            off = spot[0] if at is None else at
            if at is None:
                spot[0] += (free + 31) // 32 * 32
            assert off + free <= 229344, (name, off + free)
            return nc.alloc_sbuf_tensor_at(name, list(shape), dt, offset=off)

        x_hi = put("x_hi", [P, KB, T], F32R)
        x_lo = put("x_lo", [P, KB, T], F32R)
        raw = put("raw", [P, 2, KB, P])
        w_hi = [put(f"w_hi{s}", [P, KB, P], F32R) for s in range(2)]
        w_lo = [put(f"w_lo{s}", [P, KB, P], F32R) for s in range(2)]
        ident = put("ident", [P, P])
        ones = put("ones", [P, P])
        cmask = put("cmask", [P, P], I32)
        cmaskf = put("cmaskf", [P, P])
        keep = put("keep", [P, W])
        rb = put("rb", [P, T])
        gains = put("gains", [P, 3, KB])
        gmem = put("gmem", [P, KB])
        lbt = put("lbt", [P, 2, H])
        lbw = put("lbw", [P, 4, H])
        omlb = put("omlb", [P, H])
        hnorm = put("hnorm", [P, H])
        pscale = put("pscale", [P, H])
        ss = put("ss", [P, 16])
        eps = put("eps", [P, 1])
        pad = put("pad", [P, 4])
        rtok = put("rtok", [P, 16])
        fac = put("fac", [P, 16])
        r0 = spot[0]
        Z = T * 4

        proj = put("proj", [P, 20, T], at=r0)
        q_, f_, i_, g_, u_ = (proj[:, 4 * n:4 * n + 4, :] for n in range(5))
        y_lo = put("y_lo", [P, KB, T], F32R, at=r0)
        y_hi = put("y_hi", [P, KB, T], F32R, at=r0 + 8 * Z)
        r1 = r0 + 20 * Z
        o0 = r1
        names = ["lf", "b", "d", "e1", "e2", "e3a", "e3b", "e4", "iv", "kt", "vt", "am", "S0", "S1"]
        hg = {}
        for n in names:
            hg[n] = put(n, [P, H, P], at=o0)
            o0 += 2048
        ebs = put("ebs", [P, 2, H, 2], at=o0)
        assert o0 + 64 <= 229344
        s_old = [put(f"s_old{n}", [P, H, P], at=r1 + n * 2048) for n in range(2)]
        s_new = [put(f"s_new{n}", [P, H, P], at=r1 + 4096 + n * 2048) for n in range(2)]
        osq = put("osq", [P, T], at=r1)
        orr = put("orr", [P, T], at=r1 + Z)
        o1 = r1 + 2 * Z
        pa = put("pa", [P, TP], at=o1)
        pb = put("pb", [P, TP], at=o1 + 4096)
        pastT = put("pastT", [P, H, NS * PAST], at=o1 + 8192)
        psums = put("psums", [P, H, NS], at=o1 + 8192 + 1920)
        fs = put("fs", [P, H, NS], at=o1 + 8192 + 2048)
        past = put("past", [P, W], at=o1 + 8192 + 2176)
        utok = put("utok", [32, W], at=o1 + 8192 + 2176 + 2048)
        assert o1 + 8192 + 2176 + 4096 <= r1 + 12 * 2048
        pmix = put("pmix", [P, H, P], at=r1 + 13 * 2048)

        r2 = r0 + 16 * Z
        sqacc = put("sqacc", [P, T], at=r2)
        xnew = put("xnew", [P, 2, CH], at=r2 + Z)
        xsq = put("xsq", [P, 2, CH], at=r2 + Z + 2 * CH * 4)

        qT = put("qT", [P, KB, T], at=r0)
        o_lo = put("o_lo", [P, KB, T], F32R, at=r0)
        o_hi = put("o_hi", [P, KB, T], F32R, at=r0 + 8 * Z)
        g2 = r0 + 8 * Z
        m_hi = put("m_hi", [P, KB, M], F32R, at=g2)
        m_lo = put("m_lo", [P, KB, M], F32R, at=g2 + 8192)
        mtok = put("mtok", [P, 2, D], at=g2 + 16384)
        mf = put("mf", [P, KB, P], at=g2 + 24576)
        mjunk = put("mjunk", [P, D], at=g2 + 28672)
        knat = put("knat", [P, 2, D], at=g2 + 16384)
        kvT = put("kvT", [P, 16, M], at=r2)
        vnat = put("vnat", [P, 2, D], at=r2 + 16384)
        rbm = put("rbm", [P, M], at=r2 + 24576 + 12288)
        qs = put("qs", [P, KB, P], at=r2 + 24576)
        pr = put("pr", [P, H, XD], at=r2 + 24576 + 4096)
        prT = put("prT", [P, KB, P], at=r2 + 24576 + 8192)
        smax = put("smax", [P, H], at=r2 + 24576 + 13312)
        nmax = put("nmax", [P, H], at=r2 + 24576 + 13312 + 32)
        den = put("den", [P, H], at=r2 + 24576 + 13312 + 64)
        rden = put("rden", [P, H], at=r2 + 24576 + 13312 + 96)
        kc = [put(f"kc{n}", [P, D], at=g2 + 24576 + n * 4096) for n in range(2)]
        vc = [put(f"vc{n}", [P, D], at=r2 + 38400 + n * 4096) for n in range(2)]
        ssc = put("ssc", [P, 2, NS * H], at=r2 + 38016)
        sst = put("sst", [32, 8], at=r2 + 38272)
        ssx = put("ssx", [P, 2, H], at=r2 + 38304)
        qcol = put("qcol", [P, KB], at=r2 + 38336)
        sp_ = put("sp_", [NS * H, 2, P], at=r2 + 24576 + 12288)
        so = put("so", [NS * H, D], at=r2)
        smask = keep[:, 0:256].rearrange("p (b c) -> p b c", b=NS)
        spT = keep[:, 256:320].rearrange("p (a c) -> p a c", a=2)
        spz = keep[:, 320:384].rearrange("p (a c) -> p a c", a=2)

        s_lo = put("s_lo", [P, KB, T], F32R, at=r0)
        s_hi = put("s_hi", [P, KB, T], F32R, at=r0 + 8 * Z)
        acc = put("acc", [P, KB, T], at=r2)
        r3 = r0 + 24 * Z
        fa = put("fa", [P, T], at=r3)
        fp = put("fp", [P, 2, CH], at=r3 + Z)
        sqfin = put("sqfin", [P, T], at=r3)
        gfin = put("gfin", [P, D], at=r3 + Z + 2 * CH * 4)
        ytok = [put(f"ytok{n}", [P, D], at=r0 + 4096 * n) for n in range(3)]

        xt = [put(f"xt{n}", [P, D], at=r0 + n * 4096) for n in range(9)]
        junk = put("junk", [P, D], at=r0 + 9 * 4096)

        pm = ctx.enter_context(nc.psum_tensor("pm", [P, 8, 512], F32))
        bank = [pm[:, b, :] for b in range(8)]

        def wide(b0, n=2):
            return pm[:, b0:b0 + n, :].rearrange("p b c -> p (b c)")

        raw_in = [sem(f"raw_in{s}") for s in range(2)]
        gain_on = sem("gain_on")
        hi_made = sem("hi_made")
        lo_made = sem("lo_made")
        mm_done = sem("mm_done")
        evac = sem("evac")
        const_in = sem("const_in")
        gmix_in = sem("gmix_in")
        setup = sem("setup")
        chain = sem("chain")
        x_in = [sem(f"x_in{n}") for n in range(9)]
        x_turned = sem("x_turned")
        x_split = sem("x_split")
        x_sq = sem("x_sq")
        r_made = sem("r_made")
        r_wide = sem("r_wide")
        rb_made = sem("rb_made")
        q_act = sem("q_act")
        k_act = sem("k_act")
        lf_made = sem("lf_made")
        b_made = sem("b_made")
        d_made = sem("d_made")
        e_made = sem("e_made")
        exp_d = sem("exp_d")
        exp_e = sem("exp_e")
        exp_b = sem("exp_b")
        qk_made = sem("qk_made")
        kn_made = sem("kn_made")
        qb_made = sem("qb_made")
        iv_made = sem("iv_made")
        turned = sem("turned")
        kv_out = sem("kv_out")
        ap_done = sem("ap_done")
        masked = sem("masked")
        S1_made = sem("S1_made")
        S0_made = sem("S0_made")
        o_done = sem("o_done")
        o_out = sem("o_out")
        stored = sem("stored")
        g_act = sem("g_act")
        misc_in = sem("misc_in")
        past_in = sem("past_in")
        old_in = [sem(f"old_in{s}") for s in range(2)]
        v_wide = sem("v_wide")
        fs_made = sem("fs_made")
        new_made = sem("new_made")
        new_read = sem("new_read")
        new_out = [sem(f"new_out{s}") for s in range(2)]
        o_all = sem("o_all")
        osq_made = sem("osq_made")
        osum = sem("osum")
        orr_made = sem("orr_made")
        y_step = sem("y_step")
        ya_made = sem("ya_made")
        past_turned = sem("past_turned")
        past_made = sem("past_made")
        u_turned = sem("u_turned")
        utok_made = sem("utok_made")
        pool_step = sem("pool_step")
        pooled = sem("pooled")
        spooled = sem("spooled")
        mixed = sem("mixed")
        yb_hi = sem("yb_hi")
        yb_made = sem("yb_made")
        xsum = sem("xsum")
        xh_made = sem("xh_made")
        xl_made = sem("xl_made")
        sq_made = sem("sq_made")
        sq_added = sem("sq_added")
        sq_wide = sem("sq_wide")
        mem_in = sem("mem_in")
        mem_sq = sem("mem_sq")
        mem_turned = sem("mem_turned")
        mem_step = sem("mem_step")
        rbm_wide = sem("rbm_wide")
        rbm_made = sem("rbm_made")
        kv_turned = sem("kv_turned")
        kv_nat = sem("kv_nat")
        kn_out = sem("kn_out")
        qs_made = sem("qs_made")
        sc_done = sem("sc_done")
        mx_step = sem("mx_step")
        mx_made = sem("mx_made")
        ex_made = sem("ex_made")
        rd_made = sem("rd_made")
        p_made = sem("p_made")
        pt_done = sem("pt_done")
        pt_out = sem("pt_out")
        pv_done = sem("pv_done")
        pv_hi = sem("pv_hi")
        pv_out = sem("pv_out")
        kc_in = [sem(f"kc_in{s}") for s in range(2)]
        vc_in = [sem(f"vc_in{s}") for s in range(2)]
        qc_made = sem("qc_made")
        sq_w = sem("sq_w")
        ssx_made = sem("ssx_made")
        ssc_made = sem("ssc_made")
        sv_done = sem("sv_done")
        smask_made = sem("smask_made")
        spz_made = sem("spz_made")
        so_out = sem("so_out")
        so_turned = sem("so_turned")
        ssc_turned = sem("ssc_turned")
        ssm = sem("ssm")
        sex = sem("sex")
        sp_turned = sem("sp_turned")
        so_made = sem("so_made")
        silu_made = sem("silu_made")
        fprod = sem("fprod")
        s_hi_made = sem("s_hi_made")
        s_made = sem("s_made")
        acc_made = sem("acc_made")
        gfin_in = sem("gfin_in")
        pool_zero = sem("pool_zero")
        y_turned = sem("y_turned")
        yfac = sem("yfac")
        y_made = sem("y_made")
        fsq_made = sem("fsq_made")
        fsq_added = sem("fsq_added")
        fsum = sem("fsum")
        y_out = [sem(f"y_out{s}") for s in range(3)]
        block = ctx.enter_context(nc.Block())
        stores = [0]

        def stripe_src(p, j, s):
            name = p.name
            if name in ("qfi", "gu"):
                w, off = t["w_in"], (0 if name == "qfi" else 12 * P)
            elif name == "out":
                w, off = t["w_out"], 0
            elif name == "cq":
                w, off = t["w_cq"], 0
            elif name == "kv":
                w, off = t["w_mem_kv"], 0
            elif name == "co":
                w, off = t["w_co"], 0
            elif name.startswith("in"):
                v = t["w_ffn_in"].rearrange("(k p) n -> p k n", p=P)
                return v, int(name[2:]) * P, P, s * FF
            else:
                f0 = int(name[4:])
                fb = dict(GROUPS)[f0]
                v = t["w_ffn_out"][f0 * P:(f0 + fb) * P, :].rearrange("(k p) n -> p k n", p=P)
                return v, 0, 2 * P, s * P
            return w.rearrange("(k p) n -> p k n", p=P), off, 2 * P, s * P

        @block.sync
        def _(sp):
            def load_stripe(p, i, s, wait=True):
                v, off, step, extra = stripe_src(p, i, s)
                if wait:
                    sp.wait_ge(lo_made, p.first + 2 * i + s - 1)
                kb = v.shape[1]
                src = v[:, :, bass.ds(i * step + (off + extra), P)]
                sp.dma_start(raw[:, s, 0:kb, :], src).then_inc(raw_in[s], 16)

            for n in range(9):
                src = t["x_prompt"][0, n * P:(n + 1) * P, :] if n < 8 else t["x_sample"].rearrange("b o d -> (b o) d")
                rows = P if n < 8 else NS
                sp.dma_start(xt[n][0:rows, :], src).then_inc(x_in[n], 16)
                if n == 2:
                    sp.dma_start(gains[:, 0, :], t["g_mix"].rearrange("(k p) -> p k", p=P),
                         allow_slow_non_contiguous=True).then_inc(gmix_in, 16)
                    load_stripe(phases[0], 0, 0, False)
                    load_stripe(phases[0], 0, 1, False)
            sp.dma_start(gains[:, 1, :], t["g_cross"].rearrange("(k p) -> p k", p=P),
                         allow_slow_non_contiguous=True).then_inc(const_in, 16)
            sp.dma_start(gains[:, 2, :], t["g_ffn"].rearrange("(k p) -> p k", p=P),
                         allow_slow_non_contiguous=True).then_inc(const_in, 16)
            sp.dma_start(gmem[:, :], t["g_mem"].rearrange("(k p) -> p k", p=P),
                         allow_slow_non_contiguous=True).then_inc(const_in, 16)
            sp.dma_start(lbt[:, :, :], t["hgrn_lb"].rearrange("l (h p) -> p l h", p=P),
                         allow_slow_non_contiguous=True).then_inc(const_in, 16)
            sp.dma_start(hnorm[:, :], t["hgrn_norm"].rearrange("(h p) -> p h", p=P),
                         allow_slow_non_contiguous=True).then_inc(const_in, 16)
            sp.dma_start(pscale[:, :], t["pool_scale"].rearrange("(h p) -> p h", p=P),
                         allow_slow_non_contiguous=True).then_inc(const_in, 16)
            for p in phases:
                at = 1 if p is phases[0] else 0
                if p.name == "co":
                    at = 1
                if p.name in ("out", "cq", "kv"):
                    load_stripe(p, 0, 0)
                    load_stripe(p, 0, 1)
                    at = 1
                if p.name == "out":
                    sp.wait_ge(o_done, PAIRS + 2)
                    sp.wait_ge(S0_made, PAIRS + 1)
                    sp.dma_start(t["hgrn_prompt"][0].rearrange("h k v -> k h v"), hg["S0"][:, :, :]).then_inc(stored, 16)
                    sp.dma_start(past[0:NS * PAST, :],
                                 t["state_pool"].rearrange("b r c -> (b r) c")).then_inc(past_in, 16)
                    sp.dma_start(pmix[:, :, :], t["pool_mix"].rearrange("g c d -> c g d")).then_inc(misc_in, 16)
                    for b in range(NS):
                        if b >= 2:
                            sp.wait_ge(new_made, 2 * b - 2)
                        sp.dma_start(s_old[b % 2][:, :, :],
                                     t["state_hgrn"][b].rearrange("h k v -> k h v")).then_inc(old_in[b % 2], 16)
                if p.name == "cq":
                    sp.wait_ge(mm_done, p.done)
                    for n in range(2):
                        sp.dma_start(mtok[:, n, :], t["mem_prompt"][0, n * P:(n + 1) * P, :]).then_inc(mem_in, 16)
                def load_keys(i, s):
                    if not isinstance(i, int):
                        sp.wait_ge(ssc_made, 2 * i + s)
                    sp.dma_start(kc[s][:, :], k_rows[bass.ds(i * M + s * P, P), :]).then_inc(kc_in[s], 16)

                def load_values(n, s):
                    if not isinstance(n, int):
                        sp.wait_ge(sv_done, 2 * n + s)
                    sp.dma_start(vc[s][:, :], v_rows[bass.ds(n * M + s * P, P), :]).then_inc(vc_in[s], 16)

                if p.name == "kv":
                    k_rows = t["cache_mem_k"].rearrange("b m h d -> (b m) (h d)")
                    v_rows = t["cache_mem_v"].rearrange("b m h d -> (b m) (h d)")
                    sp.wait_ge(mem_step, 6)
                    sp.wait_ge(mem_sq, 2)
                    for s in range(2):
                        load_keys(0, s)
                if p is phases[-1]:
                    sp.dma_start(gfin[:, :], t["g_final"].unsqueeze(0).to_broadcast([P, D])).then_inc(gfin_in, 16)
                with sp.Fori(at, p.stripes // 2) as i:
                    for s in range(2):
                        load_stripe(p, i, s)
                        if p.name == "kv":
                            load_keys(i, s)
                if p.name == "kv":
                    for s in range(2):
                        load_values(0, s)
                    load_stripe(ph["co"], 0, 0)
                    load_stripe(ph["co"], 0, 1)
                    sp.wait_ge(kv_nat, 2)
                    sp.dma_start(t["mem_k"][0].rearrange("(a p) h d -> p a (h d)", p=P), knat[:, :, :]).then_inc(kn_out, 16)
                    sp.wait_ge(kv_nat, 4)
                    sp.dma_start(t["mem_v"][0].rearrange("(a p) h d -> p a (h d)", p=P), vnat[:, :, :]).then_inc(stored, 16)
                    with sp.Fori(1, NS) as n:
                        for s in range(2):
                            load_values(n, s)
            for n in range(9):
                rows = P if n < 8 else NS
                sp.wait_ge(y_made, n + 1)
                dst = t["y_prompt"][0, n * P:(n + 1) * P, :] if n < 8 else t["y_sample"].rearrange("b o d -> (b o) d")
                sp.dma_start(dst, ytok[n % 3][0:rows, :]).then_inc(y_out[n % 3], 16)
            for n in range(3):
                sp.wait_ge(y_out[n], 16 * 3)
            sp.wait_ge(new_out[0], 16 * 4)
            sp.wait_ge(new_out[1], 16 * 4)
            sp.wait_ge(kn_out, 16)
            sp.wait_ge(stored, 16 * 5)

        def nxt(p, i, s, last):
            if s == 0:
                return p, i, 1
            if not last:
                return p, i + 1, 0
            q = after.get(p.name)
            return (q, 0, 0) if q else None

        def pairs(eng, p, body):
            n = p.stripes // 2
            with eng.Fori(0, n - 1) as i:
                body(i, False)
            body(n - 1, True)

        @block.gpsimd
        def _(pool):
            pool.memset(ident[:, :], 0.0).then_inc(setup, 1)
            pool.wait_ge(setup, 1)
            pool.affine_select(out=ident[:, :], in_=ident[:, :], compare_op=ALU.not_equal, fill=1.0, base=0,
                               pattern=[[-1, P]], channel_multiplier=1).then_inc(setup, 1)
            pool.memset(ones[:, :], 1.0).then_inc(setup, 1)
            pool.memset(cmaskf[:, :], 1.0).then_inc(setup, 1)
            pool.wait_ge(setup, 4)
            pool.affine_select(out=cmaskf[:, :], in_=cmaskf[:, :], compare_op=ALU.is_ge, fill=0.0, base=0,
                               pattern=[[1, P]], channel_multiplier=-1).then_inc(setup, 1)
            pool.wait_ge(setup, 5)
            pool.memset(cmaskf[0:C, C:P], 0.0).then_inc(setup, 1)
            pool.wait_ge(setup, 6)
            pool.tensor_copy(cmask[:, :], cmaskf[:, :]).then_inc(setup, 1)
            pool.memset(keep[:, :], 1.0).then_inc(setup, 1)
            pool.wait_ge(setup, 8)
            pool.memset(keep[:, :].rearrange("p (n c) -> p n c", c=C)[:, :, 0:1], 0.0).then_inc(setup, 1)
            pool.memset(eps[:, :], EPS).then_inc(setup, 1)
            pool.memset(pad[:, :], 0.0).then_inc(sq_made, 2)

            def gain_stripe(p, i, s):
                pool.wait_ge(raw_in[s], p.first * 8 + 16 * i + 16)
                g = gains[:, p.gain, :].unsqueeze(2).to_broadcast([P, KB, P])
                pool.tensor_tensor(raw[:, s, :, :], raw[:, s, :, :], g, ALU.mult).then_inc(gain_on, 1)

            def v_copy(i, s):
                p_ = 2 * i + s
                pool.wait_ge(evac, ph["gu"].done)
                pool.wait_ge(turned, p_ + 1)
                pool.tensor_copy(hg["iv"][:, :, :], i_[:, :, bass.ds(p_ * P, P)]).then_inc(iv_made, 1)

            def pooling():
                steps = [0]

                def step(ins):
                    steps[0] += 1
                    ins.then_inc(pool_step, 1)
                    pool.wait_ge(pool_step, steps[0])

                pool.wait_ge(evac, ph["out"].done)
                pool.wait_ge(o_done, PAIRS + 2)
                pool.wait_ge(u_turned, 1)
                for g, w in enumerate(POOLW):
                    cur = u_[:, g, 0:TP]
                    for l in range(g + 1):
                        dst, sh = (pa, pb)[l % 2][:, :], 1 << l
                        step(pool.tensor_tensor(dst[:, sh:TP], cur[:, sh:TP], cur[:, 0:TP - sh], ALU.add))
                        step(pool.tensor_copy(dst[:, 0:sh], cur[:, 0:sh]))
                        cur = dst
                    for c in range(w - 1):
                        step(pool.tensor_scalar(cur[:, c:c + 1], cur[:, c:c + 1], w / (c + 1.0), None, ALU.mult))
                    step(pool.tensor_scalar(cur, cur, 1.0 / w, None, ALU.mult))
                    pool.tensor_tensor(u_[:, g, 0:TP], cur, u_[:, g, 0:TP], ALU.subtract).then_inc(pooled, 1)
                    pool.wait_ge(pooled, g + 1)

            def final_squares():
                pool.wait_ge(s_made, 3 * FB)
                pool.memset(sqfin[:, :], 0.0).then_inc(fsq_added, 1)

                def body(i, last):
                    for s in range(2):
                        for c in range(NC):
                            e = 6 * i + 3 * s + c
                            a = acc[:, bass.ds(2 * i + s, 1), c * CH:(c + 1) * CH].squeeze(1)
                            pool.wait_ge(evac, p.done + e + 1)
                            pool.wait_ge(fsq_added, e + 1)
                            pool.tensor_tensor(fp[:, c % 2, :], a, a, ALU.mult).then_inc(fsq_made, 1)
                            pool.wait_ge(fsq_made, e + 1)
                            cc = sqfin[:, c * CH:(c + 1) * CH]
                            pool.tensor_tensor(cc, cc, fp[:, c % 2, :], ALU.add).then_inc(fsq_added, 1)
                pairs(pool, p, body)

            def sample_values():
                pool.wait_ge(evac, p.done)
                pool.memset(smask[:, :, :], 0.0).then_inc(smask_made, 1)
                pool.wait_ge(smask_made, 1)
                for b in range(NS):
                    last = pool.memset(smask[:, b, b * H:(b + 1) * H], 1.0)
                last.then_inc(smask_made, 1)
                with pool.Fori(0, NS) as n:
                    pool.wait_ge(sv_done, 2 * n + 1)
                    pool.wait_ge(ssm, 5)
                    pool.wait_ge(smask_made, 2)
                    pool.tensor_tensor(spz[:, :, :], spT[:, :, :], smask[:, bass.ds(n, 1), :].to_broadcast([P, 2, NS * H]),
                                       ALU.mult).then_inc(spz_made, 1)

            def squares(p, i, s, c):
                e = 6 * i + 3 * s + c
                at = 0 if p.name == "out" else 8 * NC
                slot = (3 * s + c) % 2
                pool.wait_ge(xsum, at + e + 1)
                pool.wait_ge(setup, 10)
                pool.tensor_tensor(xsq[:, slot, :], xnew[:, slot, :], xnew[:, slot, :], ALU.mult).then_inc(sq_made, 1)
                pool.wait_ge(sq_made, at + e + 3)
                cc = sqacc[:, c * CH:(c + 1) * CH]
                pool.tensor_tensor(cc, cc, xsq[:, slot, :], ALU.add).then_inc(sq_added, 1)
                pool.wait_ge(sq_added, at + e + 1)

            for p in phases:
                if p.name == "out":
                    pooling()
                if p.name in ("out", "co"):
                    pool.wait_ge(evac, p.done + 1)
                    pool.memset(sqacc[:, :], 0.0).then_inc(pool_zero, 1)
                    pool.wait_ge(pool_zero, 1 if p.name == "out" else 2)
                    def body(i, last):
                        if last:
                            gain_stripe(after[p.name], 0, 0)
                        for s in range(2):
                            for c in range(NC):
                                squares(p, i, s, c)
                    pairs(pool, p, body)
                if p.name == "kv":
                    sample_values()
                if p is phases[-1]:
                    final_squares()
                if p.gain is None:
                    continue
                if p is phases[0]:
                    pool.wait_ge(gmix_in, 16)
                ahead = p.name in ("cq", "in0")
                if ahead:
                    gain_stripe(p, 0, 1)
                with pool.Fori(1 if ahead else 0, p.stripes // 2) as i:
                    for s in range(2):
                        gain_stripe(p, i, s)
                        if p.name == "gu":
                            v_copy(i, s)

        @block.scalar
        def _(act):
            def split_hi(p, i, s, free):
                act.wait_ge(raw_in[s], p.first * 8 + 16 * i + 16)
                if p.gain is not None:
                    act.wait_ge(gain_on, p.scaled + 2 * i + s + 1)
                if free is not None:
                    act.wait_ge(mm_done, free)
                act.activation(w_hi[s][:, :, :], raw[:, s, :, :], ACT.Copy).then_inc(hi_made, 1)

            def split_next(p, i, s, last):
                n = nxt(p, i, s, last)
                if n:
                    split_hi(*n, free=p.done + 2 * p.chunks * i + s * p.chunks)

            split_hi(phases[0], 0, 0, None)
            act.wait_ge(chain, 1)
            act.wait_ge(setup, 10)
            for n in range(9):
                rows = P if n < 8 else NS
                act.wait_ge(x_in[n], 16)
                if n:
                    act.wait_ge(x_sq, n)
                act.activation(junk[0:rows, :], xt[n][0:rows, :], ACT.Square,
                               accum_out=ss[0:rows, n:n + 1]).then_inc(x_sq, 1)
            act.wait_ge(x_sq, 9)
            act.wait_ge(o_out, 1)
            act.preload_act_table_set(LN_EXP)
            act.activation(rtok[:, 0:9], ss[:, 0:9], ACT.Ln, scale=1.0 / D, bias=eps[:, 0:1]).then_inc(x_sq, 1)
            act.wait_ge(x_sq, 10)
            act.activation(rtok[:, 0:9], rtok[:, 0:9], ACT.Exp, scale=-0.5).then_inc(r_made, 1)
            act.wait_ge(chain, 3)
            act.activation(lbw[:, 0:2, :], lbt[:, :, :], ACT.Exp).then_inc(r_made, 1)

            p = ph["qfi"]
            for i in range(6):
                for s in range(2):
                    split_next(p, i, s, i == 5)
                if i == 2:
                    act.wait_ge(evac, p.done + 12)
                    act.activation(q_, q_, ACT.Silu).then_inc(q_act, 1)
                if i == 4:
                    act.wait_ge(evac, p.done + 24)
                    act.activation(f_, f_, ACT.Sigmoid, scale=-1.0).then_inc(k_act, 1)
                    act.wait_ge(k_act, 1)
                    act.wait_ge(chain, 6)
                    for h in range(H):
                        act.activation(f_[:, h, :], f_[:, h, :], ACT.Copy, scale=omlb[:, h:h + 1]).then_inc(k_act, 1)

            def gates(i, s):
                n = 2 * i + s
                act.preload_act_table_set(LN_EXP)
                act.activation(hg["lf"][:, :, :], f_[:, :, bass.ds(n * P, P)], ACT.Ln, scale=-1.0,
                               bias=1.0).then_inc(lf_made, 1)
                act.wait_ge(e_made, n + 1)
                act.wait_ge(turned, n + 1)
                act.activation(hg["e4"][:, :, :], hg["lf"][:, :, :], ACT.Exp).then_inc(exp_e, 1)
                act.wait_ge(o_done, n + 1)
                if not isinstance(n, int) or n:
                    act.wait_ge(S0_made, n)
                act.activation(ebs[:, s, :, :], hg["b"][:, :, C - 1::C], ACT.Exp)
                act.activation(hg["e3a" if s == 0 else "e3b"][:, :, :], hg["b"][:, :, :], ACT.Exp).then_inc(exp_b, 1)
                act.wait_ge(d_made, n + 1)
                act.wait_ge(ap_done, n + 1)
                act.activation(hg["e1"][:, :, :], hg["d"][:, :, :], ACT.Exp)
                act.activation(hg["e2"][:, :, :], hg["d"][:, :, :], ACT.Exp, scale=-1.0).then_inc(exp_d, 1)

            def kv_read(i, s):
                n = 2 * i + s
                act.wait_ge(turned, n + 2)
                act.wait_ge(o_done, n + 2)
                act.activation(hg["kt"][:, :, :], bank[3].rearrange("p (h c) -> p h c", h=H), ACT.Copy)
                act.activation(hg["vt"][:, :, :], bank[4].rearrange("p (h c) -> p h c", h=H),
                               ACT.Copy).then_inc(kv_out, 1)

            act.wait_ge(k_act, 1 + H)
            gates(0, 0)
            p = ph["gu"]

            def gu_body(i, last):
                for s in range(2):
                    split_next(p, i, s, last)
                    kv_read(i, s)
                    n = nxt(p, i, s, last)
                    if n and n[0] is p:
                        gates(n[1], n[2])
            pairs(act, p, gu_body)

            def mixer_end():
                act.wait_ge(evac, ph["gu"].done + 4 * NC)
                act.activation(g_, g_, ACT.Sigmoid).then_inc(g_act, 1)
                act.wait_ge(past_turned, 1)
                act.wait_ge(o_done, PAIRS + 2)
                act.activation(pastT[:, :, :], bank[5][:, 0:480].rearrange("p (g r) -> p g r", g=H),
                               ACT.Copy).then_inc(past_made, 1)
                act.wait_ge(u_turned, 1)
                act.activation(utok[0:23, :], bank[3][0:23, :], ACT.Copy).then_inc(utok_made, 1)
                act.wait_ge(utok_made, 1)
                act.dma_start(t["pool_prompt"][0], utok[0:PAST, :]).then_inc(stored, 16)
                act.dma_start(t["pool_sample"][:, PAST - 1, :], utok[PAST:PAST + NS, :]).then_inc(stored, 16)
                act.dma_start(t["pool_sample"][:, 0:PAST - 1, :], t["state_pool"][:, 1:PAST, :]).then_inc(stored, 16)
                for b in range(NS):
                    act.wait_ge(new_made, 2 * b + 2)
                    act.dma_start(t["hgrn_sample"][b].rearrange("h k v -> k h v"),
                                  s_new[b % 2][:, :, :]).then_inc(new_out[b % 2], 16)
                act.preload_act_table_set(LN_EXP)
                act.wait_ge(o_all, 1)
                act.wait_ge(new_out[0], 16 * 4)
                act.wait_ge(new_out[1], 16 * 4)
                for h in range(H):
                    if h:
                        act.wait_ge(osum, h)
                    act.activation(osq[:, :], q_[:, h, :], ACT.Square).then_inc(osq_made, 1)
                    act.wait_ge(osum, h + 1)
                    if h:
                        act.wait_ge(y_step, 3 * h - 2)
                    o3 = orr[:, :].rearrange("p (c n) -> p c n", c=NC)
                    act.activation(o3, pm[:, 3:6, 0:CH], ACT.Ln, scale=1.0 / P, bias=eps[:, 0:1]).then_inc(orr_made, 1)
                    act.wait_ge(orr_made, 2 * h + 1)
                    act.activation(o3, o3, ACT.Exp, scale=-0.5).then_inc(orr_made, 1)
                for g in range(H):
                    for c in range(NC):
                        e = 3 * g + c
                        act.wait_ge(mixed, e + 1)
                        act.wait_ge(ya_made, g + 1)
                        act.activation(y_hi[:, 4 + g, c * CH:(c + 1) * CH], bank[3 + e % 3][:, 0:CH], ACT.Copy,
                                       scale=pscale[:, g:g + 1]).then_inc(yb_hi, 1)

            def norm_factors(n):
                act.preload_act_table_set(LN_EXP)
                act.wait_ge(sq_wide, n)
                r3_ = rb[:, :].rearrange("p (c n) -> p c n", c=NC)
                act.wait_ge(evac, ph["cq"].done if n == 1 else ph["in0"].done)
                act.activation(r3_, pm[:, 3:6, 0:CH], ACT.Ln, scale=1.0 / D, bias=eps[:, 0:1]).then_inc(rb_made, 1)
                act.wait_ge(rb_made, 2 * n)
                act.activation(r3_, r3_, ACT.Exp, scale=-0.5).then_inc(rb_made, 1)

            def split_only(p):
                def body(i, last):
                    for s in range(2):
                        split_next(p, i, s, last)
                pairs(act, p, body)

            def memory_in():
                for n in range(2):
                    act.wait_ge(mem_in, 32)
                    if n:
                        act.wait_ge(mem_sq, n)
                    act.activation(mjunk[:, :], mtok[:, n, :], ACT.Square,
                                   accum_out=ss[:, 9 + n:10 + n]).then_inc(mem_sq, 1)
                act.wait_ge(mem_sq, 2)
                act.activation(rtok[:, 9:11], ss[:, 9:11], ACT.Ln, scale=1.0 / D, bias=eps[:, 0:1]).then_inc(mem_sq, 1)
                act.wait_ge(mem_sq, 3)
                act.activation(rtok[:, 9:11], rtok[:, 9:11], ACT.Exp, scale=-0.5).then_inc(mem_sq, 1)

            def q_block(n):
                if not isinstance(n, int) or n:
                    act.wait_ge(sc_done, n)
                act.wait_ge(evac, ph["kv"].done)
                act.activation(qs[:, :, :], qT[:, :, bass.ds(n * P, P)], ACT.Copy).then_inc(qs_made, 1)

            def exps(n):
                act.wait_ge(mx_made, n + 1)
                if not isinstance(n, int) or n:
                    act.wait_ge(pt_done, n)
                for h in range(H):
                    last = act.activation(pr[:, h, :], wide(0)[:, h * XD:(h + 1) * XD], ACT.Exp, scale=SCALE,
                                          bias=nmax[:, h:h + 1], accum_out=den[:, h:h + 1])
                last.then_inc(ex_made, 1)

            def sample_q(b):
                if not isinstance(b, int):
                    act.wait_ge(sq_w, b)
                act.wait_ge(evac, ph["kv"].done)
                act.activation(qcol[:, :].unsqueeze(2), qT[:, :, bass.ds(TP + b, 1)], ACT.Copy).then_inc(qc_made, 1)

            def keys_values(p):
                sample_q(0)

                def body(i, last):
                    split_next(p, i, 0, last)
                    if not last:
                        sample_q(i + 1)
                    split_next(p, i, 1, last)
                pairs(act, p, body)

            def attention():
                q_block(0)
                sample_softmax()
                exps(0)

                def body(n, more):
                    if more:
                        q_block(n + 1)
                    act.wait_ge(pt_done, n + 1)
                    act.wait_ge(pv_done, n + 1)
                    act.activation(prT[:, :, :], wide(2).rearrange("p (k c) -> p k c", k=KB), ACT.Copy).then_inc(pt_out, 1)
                    if more:
                        exps(n + 1)
                with act.Fori(0, PAIRS - 1) as n:
                    body(n, True)
                body(PAIRS - 1, False)

            def sample_softmax():
                act.wait_ge(ssm, 2)
                act.activation(sp_[:, :, :], bank[7][0:32, 0:M].rearrange("p (a c) -> p a c", a=2), ACT.Exp, scale=SCALE,
                               bias=sst[:, 1:2], accum_out=sst[:, 2:3]).then_inc(sex, 1)

            for p in phases[2:]:
                if p.name == "out":
                    mixer_end()
                    split_only(p)
                    norm_factors(1)
                elif p.name == "cq":
                    split_only(p)
                    memory_in()
                elif p.name == "kv":
                    keys_values(p)
                    attention()
                    act.wait_ge(sv_done, 2 * NS + 1)
                    act.activation(so[:, :], wide(6)[0:NS * H, :], ACT.Copy).then_inc(so_out, 1)
                elif p.name == "co":
                    split_only(p)
                    norm_factors(2)
                elif p.name.startswith("in"):
                    g0 = int(p.name[2:])

                    def body(i, last):
                        split_next(p, i, 0, last)
                        for c in range(NC):
                            act.wait_ge(evac, p.done + 6 * i + c + 1)
                            cc = fa[:, c * CH:(c + 1) * CH]
                            act.activation(cc, cc, ACT.Silu).then_inc(silu_made, 1)
                            if c == 1:
                                split_next(p, i, 1, last)
                    pairs(act, p, body)
                else:
                    split_only(p)
            act.preload_act_table_set(LN_EXP)
            act.wait_ge(fsum, 1)
            for rows, cols in ((P, slice(0, 8)), (NS, slice(8, 9))):
                last = act.activation(fac[0:rows, cols], bank[7][0:rows, cols], ACT.Ln, scale=1.0 / D,
                                      bias=eps[0:rows, 0:1])
            last.then_inc(yfac, 1)
            act.wait_ge(yfac, 1)
            for rows, cols in ((P, slice(0, 8)), (NS, slice(8, 9))):
                last = act.activation(fac[0:rows, cols], fac[0:rows, cols], ACT.Exp, scale=-0.5)
            last.then_inc(yfac, 1)

        @block.vector
        def _(dve):
            dve.memset(ss[:, :], 1.0).then_inc(chain, 1)
            dve.memset(fac[:, 1:16], 0.0).then_inc(evac, 4)
            dve.memset(rtok[:, :], 0.0).then_inc(o_out, 1)
            dve.memset(fac[:, 0:1], 0.0).then_inc(pv_out, 1)

            def split_lo(n_):
                p, i, s = n_
                dve.wait_ge(hi_made, p.first + 2 * i + s + 1)
                dve.tensor_tensor(w_lo[s][:, :, :], raw[:, s, :, :], w_hi[s][:, :, :].bitcast(F32),
                                  ALU.subtract).then_inc(lo_made, 1)

            for n in range(9):
                cols = P if n < 8 else NS
                dve.wait_ge(x_turned, n + 1)
                src = wide(3 + 2 * (n % 2)).rearrange("p (k c) -> p k c", k=KB)[:, :, 0:cols]
                h_, l_ = x_hi[:, :, n * P:n * P + cols], x_lo[:, :, n * P:n * P + cols]
                dve.tensor_copy(h_, src).then_inc(x_split, 1)
                dve.wait_ge(x_split, 2 * n + 1)
                dve.tensor_tensor(l_, src, h_.bitcast(F32), ALU.subtract).then_inc(x_split, 1)
            split_lo((phases[0], 0, 0))
            dve.wait_ge(r_wide, 1)
            dve.tensor_copy(rb[:, :], wide(5, 3)[:, 0:T]).then_inc(rb_made, 1)
            dve.wait_ge(const_in, 16 * 6)
            dve.tensor_tensor(lbw[:, 2, :], lbt[:, 0, :], lbt[:, 1, :], ALU.max).then_inc(chain, 1)
            dve.wait_ge(chain, 2)
            dve.tensor_tensor(lbt[:, :, :], lbt[:, :, :], lbw[:, 2:3, :].to_broadcast([P, 2, H]),
                              ALU.subtract).then_inc(chain, 1)
            dve.wait_ge(r_made, 2)
            dve.tensor_tensor(lbw[:, 2, :], lbw[:, 0, :], lbw[:, 1, :], ALU.add).then_inc(chain, 1)
            dve.wait_ge(chain, 4)
            dve.reciprocal(lbw[:, 3, :], lbw[:, 2, :]).then_inc(chain, 1)
            dve.wait_ge(chain, 5)
            dve.tensor_tensor(omlb[:, :], lbw[:, 1, :], lbw[:, 3, :], ALU.mult).then_inc(chain, 1)
            dve.wait_ge(rb_made, 1)

            def plain_evac(p, i, s, c, dst):
                dve.wait_ge(mm_done, p.done + 6 * i + 3 * s + c + 1)
                dve.tensor_tensor(dst, bank[c][:, 0:CH], rb[:, c * CH:(c + 1) * CH], ALU.mult).then_inc(evac, 1)

            def qfi_body(i, last):
                p = ph["qfi"]
                for s in range(2):
                    for c in range(NC):
                        plain_evac(p, i, s, c, proj[:, bass.ds(2 * i + s, 1), c * CH:(c + 1) * CH].squeeze(1))
                        if c == 0:
                            n = nxt(p, i, s, last)
                            if n:
                                split_lo(n)
            pairs(dve, ph["qfi"], qfi_body)

            def flat(x):
                return x[:, :, :].rearrange("p h c -> p (h c)")

            def decays(i, s):
                n = 2 * i + s
                dve.wait_ge(lf_made, n + 1)
                dve.tensor_tensor_scan(flat(hg["b"]), keep[:, :], flat(hg["lf"]), 0.0, ALU.mult,
                                       ALU.add).then_inc(b_made, 1)
                dve.wait_ge(b_made, n + 1)
                b4 = flat(hg["b"]).rearrange("p (n c) -> p n c", c=C)
                dve.tensor_tensor(flat(hg["lf"]).rearrange("p (n c) -> p n c", c=C),
                                  b4[:, :, C - 1:C].to_broadcast([P, 8, C]), b4, ALU.subtract).then_inc(e_made, 1)
                dve.tensor_tensor(flat(hg["d"]).rearrange("p (n c) -> p n c", c=C), b4,
                                  b4[:, :, MID:MID + 1].to_broadcast([P, 8, C]), ALU.subtract).then_inc(d_made, 1)

            def weigh(i, s):
                n = 2 * i + s
                qv, kv = q_[:, :, bass.ds(n * P, P)], f_[:, :, bass.ds(n * P, P)]
                e3 = hg["e3a" if s == 0 else "e3b"]
                dve.wait_ge(exp_e, n + 1)
                dve.tensor_tensor(hg["e4"][:, :, :], hg["e4"][:, :, :], kv, ALU.mult).then_inc(kn_made, 1)
                dve.wait_ge(exp_b, n + 1)
                dve.tensor_tensor(e3[:, :, :], e3[:, :, :], qv, ALU.mult).then_inc(qb_made, 1)
                dve.wait_ge(exp_d, n + 1)
                dve.tensor_tensor(hg["e1"][:, :, :], hg["e1"][:, :, :], qv, ALU.mult)
                dve.tensor_tensor(hg["e2"][:, :, :], hg["e2"][:, :, :], kv, ALU.mult).then_inc(qk_made, 1)

            def mask(i, s):
                dve.copy_predicated(hg["am"][:, :, :], cmask[:, :].unsqueeze(1).to_broadcast([P, H, P]),
                                    bank[5].rearrange("p (h c) -> p h c", h=H)).then_inc(masked, 1)

            def state(i, s, x):
                a, b_ = (hg["S0"], hg["S1"]) if x == 0 else (hg["S1"], hg["S0"])
                n = 2 * i + s
                if x == 0:
                    dve.wait_ge(ap_done, n + 2)
                    dve.wait_ge(o_done, n + 2)
                    dve.wait_ge(S0_made, n + 1)
                else:
                    dve.wait_ge(S1_made, n + 1)
                for h in range(H):
                    last = dve.scalar_tensor_tensor(b_[:, h, :], a[:, h, :], ebs[:, s, h, x:x + 1],
                                                    bank[6 + x][:, h * P:(h + 1) * P], ALU.mult, ALU.add)
                last.then_inc(S1_made if x == 0 else S0_made, 1)

            def outputs(i, s):
                n = 2 * i + s
                dve.wait_ge(o_done, n + 3)
                dve.tensor_scalar(q_[:, :, bass.ds(n * P, P)], bank[3].rearrange("p (h c) -> p h c", h=H), 1.0, None,
                                  ALU.mult).then_inc(o_out, 1)

            dve.memset(hg["am"][:, :, :], 0.0).then_inc(masked, 1)
            dve.memset(hg["S0"][:, :, :], 0.0).then_inc(S0_made, 1)
            dve.wait_ge(q_act, 1)
            dve.wait_ge(masked, 1)
            decays(0, 0)
            weigh(0, 0)
            p = ph["gu"]

            def gu_body(i, last):
                for s in range(2):
                    n = nxt(p, i, s, last)
                    dst = proj[:, bass.ds(12 + 2 * i + s, 1), :].squeeze(1)
                    more = n and n[0] is p
                    plain_evac(p, i, s, 0, dst[:, 0:CH])
                    if n:
                        split_lo(n)
                    if more:
                        decays(n[1], n[2])
                    plain_evac(p, i, s, 1, dst[:, CH:2 * CH])
                    state(i, s, 0)
                    mask(i, s)
                    plain_evac(p, i, s, 2, dst[:, 2 * CH:T])
                    outputs(i, s)
                    state(i, s, 1)
                    if more:
                        weigh(n[1], n[2])
            pairs(dve, p, gu_body)

            def mixer_end():
                dve.wait_ge(o_done, PAIRS + 2)
                dve.tensor_scalar(fs[:, :, :], f_[:, :, TP:T], -1.0, 1.0, ALU.mult, ALU.add).then_inc(fs_made, 1)
                dve.wait_ge(fs_made, 1)
                for b in range(NS):
                    so, sn, at_b = s_old[b % 2], s_new[b % 2], slice(TP + b, TP + b + 1)
                    dve.wait_ge(old_in[b % 2], 16 * (b // 2 + 1))
                    dve.tensor_tensor(so[:, :, :], so[:, :, :], fs[:, :, b:b + 1].to_broadcast([P, H, P]),
                                      ALU.mult).then_inc(fs_made, 1)
                    dve.wait_ge(v_wide, b + 1)
                    if b >= 2:
                        dve.wait_ge(new_out[b % 2], 16 * (b // 2))
                        dve.wait_ge(new_read, b - 1)
                    dve.tensor_tensor(sn[:, :, :], bank[6 + b % 2].rearrange("p (h v) -> p h v", h=H),
                                      f_[:, :, at_b].to_broadcast([P, H, P]), ALU.mult).then_inc(new_made, 1)
                    dve.wait_ge(fs_made, b + 2)
                    dve.wait_ge(new_made, 2 * b + 1)
                    dve.tensor_tensor(sn[:, :, :], sn[:, :, :], so[:, :, :], ALU.add).then_inc(new_made, 1)
                dve.wait_ge(past_made, 1)
                dve.wait_ge(u_turned, 1)
                for g, w in enumerate(POOLW):
                    us = u_[:, g, TP:T]
                    rows = pastT[:, g, :].rearrange("p (b r) -> p b r", b=NS)[:, :, PAST - (w - 1):PAST]
                    dve.tensor_reduce(psums[:, g, :], rows, AX_X, ALU.add).then_inc(spooled, 1)
                    dve.wait_ge(spooled, 3 * g + 1)
                    dve.tensor_tensor(psums[:, g, :], psums[:, g, :], us, ALU.add).then_inc(spooled, 1)
                    dve.wait_ge(spooled, 3 * g + 2)
                    dve.scalar_tensor_tensor(us, psums[:, g, :], 1.0 / w, us, ALU.mult, ALU.subtract).then_inc(spooled, 1)
                dve.wait_ge(new_read, NS)
                dve.tensor_copy(q_[:, :, TP:T], bank[4][:, 0:H * NS].rearrange("p (h b) -> p h b", h=H)).then_inc(o_all, 1)
                dve.wait_ge(o_all, 1)
                dve.wait_ge(g_act, 1)
                for h in range(H):
                    o = q_[:, h, :]
                    dve.wait_ge(orr_made, 2 * h + 2)
                    dve.scalar_tensor_tensor(o, o, hnorm[:, h:h + 1], orr[:, :], ALU.mult, ALU.mult).then_inc(y_step, 1)
                    dve.wait_ge(y_step, 3 * h + 1)
                    dve.tensor_tensor(o, o, g_[:, h, :], ALU.mult).then_inc(y_step, 1)
                    dve.wait_ge(y_step, 3 * h + 2)
                    dve.tensor_copy(y_hi[:, h, :], o).then_inc(y_step, 1)
                    dve.wait_ge(y_step, 3 * h + 3)
                    dve.tensor_tensor(y_lo[:, h, :], o, y_hi[:, h, :].bitcast(F32), ALU.subtract).then_inc(ya_made, 1)
                for g in range(H):
                    for c in range(NC):
                        e = 3 * g + c
                        dve.wait_ge(yb_hi, e + 1)
                        dve.scalar_tensor_tensor(y_lo[:, 4 + g, c * CH:(c + 1) * CH], bank[3 + e % 3][:, 0:CH],
                                                 pscale[:, g:g + 1], y_hi[:, 4 + g, c * CH:(c + 1) * CH].bitcast(F32),
                                                 ALU.mult, ALU.subtract).then_inc(yb_made, 1)

            def residual(p):
                at = 0 if p.name == "out" else 8 * NC

                def body(i, last):
                    for s in range(2):
                        for c in range(NC):
                            e = 6 * i + 3 * s + c
                            xn = xnew[:, (3 * s + c) % 2, :]
                            xh = x_hi[:, bass.ds(2 * i + s, 1), c * CH:(c + 1) * CH].squeeze(1)
                            xl = x_lo[:, bass.ds(2 * i + s, 1), c * CH:(c + 1) * CH].squeeze(1)
                            dve.wait_ge(sq_made, at + e + 1)
                            dve.wait_ge(mm_done, p.done + e + 1)
                            dve.tensor_tensor(xn, bank[c][:, 0:CH], xh.bitcast(F32), ALU.add).then_inc(evac, 1)
                            dve.wait_ge(evac, p.done + e + 1)
                            dve.tensor_tensor(xn, xn, xl.bitcast(F32), ALU.add).then_inc(xsum, 1)
                            dve.wait_ge(xsum, at + e + 1)
                            dve.tensor_scalar(xh, xn, 1.0, None, ALU.mult).then_inc(xh_made, 1)
                            dve.wait_ge(xh_made, at + e + 1)
                            dve.tensor_tensor(xl, xn, xh.bitcast(F32), ALU.subtract).then_inc(xl_made, 1)
                            if c == 0:
                                n = nxt(p, i, s, last)
                                if n:
                                    split_lo(n)
                pairs(dve, p, body)

            def queries(p):
                dve.wait_ge(rb_made, 3)

                def body(i, last):
                    for s in range(2):
                        for c in range(NC):
                            plain_evac(p, i, s, c, qT[:, bass.ds(2 * i + s, 1), c * CH:(c + 1) * CH].squeeze(1))
                            if c == 0:
                                n = nxt(p, i, s, last)
                                if n:
                                    split_lo(n)
                pairs(dve, p, body)
                for n in range(2):
                    dve.wait_ge(mem_turned, n + 1)
                    if n:
                        dve.wait_ge(mem_step, 3)
                    dve.tensor_tensor(mf[:, :, :], wide(3 + 2 * n).rearrange("p (k c) -> p k c", k=KB),
                                      gmem[:, :].unsqueeze(2).to_broadcast([P, KB, P]), ALU.mult).then_inc(mem_step, 1)
                    dve.wait_ge(mem_step, 3 * n + 1)
                    mh, ml = m_hi[:, :, n * P:(n + 1) * P], m_lo[:, :, n * P:(n + 1) * P]
                    dve.tensor_copy(mh, mf[:, :, :]).then_inc(mem_step, 1)
                    dve.wait_ge(mem_step, 3 * n + 2)
                    dve.tensor_tensor(ml, mf[:, :, :], mh.bitcast(F32), ALU.subtract).then_inc(mem_step, 1)
                dve.wait_ge(rbm_wide, 1)
                dve.tensor_copy(rbm[:, :], bank[7][:, 0:M]).then_inc(rbm_made, 1)
                dve.wait_ge(rbm_made, 1)

            def keys_values(p):
                def sample_scores(i, s):
                    dve.wait_ge(sq_w, i + 1)
                    dve.wait_ge(kc_in[s], 16 * i + 16)
                    dve.wait_ge(ssc_made, 2 * i + s + 1)
                    dve.wait_ge(setup, 10)
                    for h in range(H):
                        kk = kc[s][:, h * XD:(h + 1) * XD]
                        last = dve.tensor_tensor_reduce(kk, kk, wide(2)[:, h * XD:(h + 1) * XD], 1.0, 0.0,
                                                        ALU.mult, ALU.add, ssx[:, s, h:h + 1])
                    last.then_inc(ssx_made, 1)
                    dve.wait_ge(ssx_made, 2 * i + s + 1)
                    dve.tensor_scalar(ssc[:, s, bass.ds(i * H, H)], ssx[:, s, :], 1.0, None, ALU.mult).then_inc(ssc_made, 1)

                def body(i, last):
                    for s in range(2):
                        n = nxt(p, i, s, last)
                        if n:
                            split_lo(n)
                        sample_scores(i, s)
                        dve.wait_ge(mm_done, p.done + 2 * i + s + 1)
                        dve.tensor_tensor(kvT[:, bass.ds(2 * i + s, 1), :].squeeze(1), bank[s][:, 0:M], rbm[:, :],
                                          ALU.mult).then_inc(evac, 1)
                pairs(dve, p, body)
                for x in range(4):
                    dve.wait_ge(kv_turned, x + 1)
                    dve.tensor_copy((knat, vnat)[x // 2][:, x % 2, :], wide(3 + 2 * (x % 2))).then_inc(kv_nat, 1)
                    if x == 1:
                        dve.wait_ge(ssc_turned, 1)
                        dve.tensor_reduce(sst[:, 0:1], bank[7][0:32, 0:M], AX_X, ALU.max).then_inc(ssm, 1)
                        dve.wait_ge(ssm, 1)
                        dve.tensor_scalar(sst[:, 1:2], sst[:, 0:1], -SCALE, None, ALU.mult).then_inc(ssm, 1)
                dve.wait_ge(sex, 1)
                dve.reciprocal(sst[:, 3:4], sst[:, 2:3]).then_inc(ssm, 1)
                dve.wait_ge(ssm, 3)
                dve.tensor_scalar(sp_[:, :, :], sp_[:, :, :], sst[:, 3:4], None, ALU.mult).then_inc(ssm, 1)

            def attention():
                def maxima(n):
                    dve.wait_ge(sc_done, n + 1)
                    dve.tensor_reduce(smax[:, :], wide(0).rearrange("p (h m) -> p h m", h=H), AX_X,
                                      ALU.max).then_inc(mx_step, 1)
                    dve.wait_ge(mx_step, n + 1)
                    dve.tensor_scalar(nmax[:, :], smax[:, :], -SCALE, None, ALU.mult).then_inc(mx_made, 1)

                def normalize(n):
                    dve.wait_ge(ex_made, n + 1)
                    dve.reciprocal(rden[:, :], den[:, :]).then_inc(rd_made, 1)
                    dve.wait_ge(rd_made, n + 1)
                    dve.tensor_tensor(pr[:, :, :], pr[:, :, :], rden[:, :].unsqueeze(2).to_broadcast([P, H, XD]),
                                      ALU.mult).then_inc(p_made, 1)

                def outputs_(n):
                    dve.wait_ge(pv_done, n + 2)
                    src = wide(4).rearrange("p (k c) -> p k c", k=KB)
                    oh = o_hi[:, :, bass.ds(n * P, P)]
                    dve.tensor_scalar(oh, src, 1.0, None, ALU.mult).then_inc(pv_hi, 1)
                    dve.wait_ge(pv_hi, n + 1)
                    dve.tensor_tensor(o_lo[:, :, bass.ds(n * P, P)], src, oh.bitcast(F32), ALU.subtract).then_inc(pv_out, 1)

                maxima(0)
                dve.wait_ge(sp_turned, 1)
                dve.tensor_copy(spT[:, :, :], bank[7][:, 256:320].rearrange("p (a b) -> p a b", a=2)).then_inc(ssm, 1)
                normalize(0)
                dve.wait_ge(kn_out, 16)
                with dve.Fori(0, PAIRS - 1) as n:
                    maxima(n + 1)
                    normalize(n + 1)
                    outputs_(n)
                outputs_(PAIRS - 1)
                dve.wait_ge(so_turned, 1)
                src = bank[0][:, 0:256].rearrange("p (k b h) -> p k b h", k=KB, h=H)
                for h in range(H):
                    last = dve.tensor_copy(o_hi[:, 2 * h:2 * h + 2, TP:T], src[:, 2 * h:2 * h + 2, :, h])
                last.then_inc(so_made, 1)
                dve.wait_ge(so_made, 1)
                for h in range(H):
                    last = dve.tensor_tensor(o_lo[:, 2 * h:2 * h + 2, TP:T], src[:, 2 * h:2 * h + 2, :, h],
                                             o_hi[:, 2 * h:2 * h + 2, TP:T].bitcast(F32), ALU.subtract)
                last.then_inc(so_made, 1)

            def ffn_in(p):
                f0 = int(p.name[2:])

                def body(i, last):
                    for c in range(NC):
                        plain_evac(p, i, 0, c, fa[:, c * CH:(c + 1) * CH])
                        if c == 0:
                            split_lo(nxt(p, i, 0, last))
                    for c in range(NC):
                        plain_evac(p, i, 1, c, fp[:, c % 2, :])
                        n = 3 * (f0 + i) + c + 1
                        dve.wait_ge(evac, p.done + 6 * i + 3 + c + 1)
                        dve.wait_ge(silu_made, n)
                        dve.tensor_tensor(fp[:, c % 2, :], fp[:, c % 2, :], fa[:, c * CH:(c + 1) * CH],
                                          ALU.mult).then_inc(fprod, 1)
                        sh = s_hi[:, bass.ds(i, 1), c * CH:(c + 1) * CH].squeeze(1)
                        sl = s_lo[:, bass.ds(i, 1), c * CH:(c + 1) * CH].squeeze(1)
                        dve.wait_ge(fprod, n)
                        dve.tensor_scalar(sh, fp[:, c % 2, :], 1.0, None, ALU.mult).then_inc(s_hi_made, 1)
                        dve.wait_ge(s_hi_made, n)
                        dve.tensor_tensor(sl, fp[:, c % 2, :], sh.bitcast(F32), ALU.subtract).then_inc(s_made, 1)
                        if c == 0:
                            split_lo(nxt(p, i, 1, last))
                pairs(dve, p, body)

            def ffn_down(p):
                first = p.name == "down0"
                if not first:
                    dve.wait_ge(acc_made, 8 * NC)
                    dve.wait_ge(evac, p.done)

                def body(i, last):
                    for s in range(2):
                        for c in range(NC):
                            e = 6 * i + 3 * s + c
                            at_ = (bass.ds(2 * i + s, 1), slice(c * CH, (c + 1) * CH))
                            a = acc[:, at_[0], at_[1]].squeeze(1)
                            dve.wait_ge(mm_done, p.done + e + 1)
                            add = x_hi[:, at_[0], at_[1]].squeeze(1).bitcast(F32) if first else a
                            dve.tensor_tensor(a, bank[c][:, 0:CH], add, ALU.add).then_inc(evac, 1)
                            if first:
                                dve.wait_ge(evac, p.done + e + 1)
                                dve.tensor_tensor(a, a, x_lo[:, at_[0], at_[1]].squeeze(1).bitcast(F32),
                                                  ALU.add).then_inc(acc_made, 1)
                            if c == 0:
                                n = nxt(p, i, s, last)
                                if n:
                                    split_lo(n)
                pairs(dve, p, body)

            for p in phases[2:]:
                if p.name == "out":
                    mixer_end()
                    residual(p)
                elif p.name == "cq":
                    queries(p)
                elif p.name == "kv":
                    keys_values(p)
                    attention()
                elif p.name == "co":
                    residual(p)
                    dve.wait_ge(rb_made, 5)
                elif p.name.startswith("in"):
                    ffn_in(p)
                else:
                    ffn_down(p)
            dve.wait_ge(gfin_in, 16)
            dve.wait_ge(yfac, 2)
            for n in range(9):
                rows = P if n < 8 else NS
                dve.wait_ge(y_turned, n + 1)
                if n >= 3:
                    dve.wait_ge(y_out[n % 3], 16 * (n // 3))
                dve.scalar_tensor_tensor(ytok[n % 3][0:rows, :], wide(Y_BANKS[n % 3])[0:rows, :],
                                         fac[0:rows, n:n + 1], gfin[0:rows, :], ALU.mult, ALU.mult).then_inc(y_made, 1)

        @block.tensor
        def _(pe):
            def stripe_chunk(p, i, s, c, hi, lo, kb=KB, cols=CH, out=None):
                out = bank[c][:, 0:cols] if out is None else out
                x0 = c * CH
                for k in range(kb):
                    pe.matmul(out, w_hi[s][:, k, :], hi[:, k, x0:x0 + cols], start=(k == 0), stop=False)
                    pe.matmul(out, w_hi[s][:, k, :], lo[:, k, x0:x0 + cols], start=False, stop=False)
                    last = pe.matmul(out, w_lo[s][:, k, :], hi[:, k, x0:x0 + cols], start=False, stop=(k == kb - 1))
                last.then_inc(mm_done, 1)

            def chunk(p, i, s, c, hi, lo, kb=KB):
                if c == 0:
                    pe.wait_ge(lo_made, p.first + 2 * i + s + 1)
                pe.wait_ge(evac, p.done + 6 * i + 3 * s - 2 + c)
                stripe_chunk(p, i, s, c, hi, lo, kb)

            pe.wait_ge(setup, 10)
            for n in range(9):
                rows = P if n < 8 else NS
                pe.wait_ge(x_in[n], 16)
                if n >= 2:
                    pe.wait_ge(x_split, 2 * (n - 1))
                for k in range(KB):
                    last = pe.transpose(wide(3 + 2 * (n % 2))[:, k * P:k * P + rows],
                                        xt[n][0:rows, k * P:(k + 1) * P], ident[0:rows, 0:rows])
                    if n == 0 and k < 6:
                        last.then_inc((mm_done, turned, ap_done, o_done, pv_done, ssc_made)[k], (4, 1, 1, 2, 1, 1)[k])
                last.then_inc(x_turned, 1)
            pe.wait_ge(x_split, 18)
            pe.wait_ge(r_made, 1)
            for n in range(9):
                cols = P if n < 8 else NS
                last = pe.matmul(wide(5, 3)[:, n * P:n * P + cols], rtok[:, n:n + 1].to_broadcast([P, P]),
                                 ident[:, 0:cols], start=True, stop=True)
            last.then_inc(r_wide, 1)

            with pe.Fori(0, 6) as i:
                for s in range(2):
                    for c in range(NC):
                        chunk(ph["qfi"], i, s, c, x_hi, x_lo)

            def turn(i, s):
                n = 2 * i + s
                pe.wait_ge(kn_made, n + 1)
                pe.wait_ge(iv_made, n + 1)
                pe.wait_ge(o_out, n + 1)
                for h in range(H):
                    pe.transpose(bank[3][:, h * P:(h + 1) * P], hg["e4"][:, h, :], ident[:, :])
                for h in range(H):
                    last = pe.transpose(bank[4][:, h * P:(h + 1) * P], hg["iv"][:, h, :], ident[:, :])
                last.then_inc(turned, 1)

            def scores(i, s):
                n = 2 * i + s
                pe.wait_ge(qk_made, n + 1)
                pe.wait_ge(kv_out, n + 1)
                pe.wait_ge(masked, n + 1)
                pe.wait_ge(S0_made, n + 1)
                for h in range(H):
                    pe.matmul(bank[5][:, h * P:(h + 1) * P], hg["e2"][:, h, :], hg["e1"][:, h, :], start=True, stop=True)
                for x in range(2):
                    for h in range(H):
                        last = pe.matmul(bank[6 + x][:, h * P:(h + 1) * P], hg["kt"][x * C:(x + 1) * C, h, :],
                                         hg["vt"][x * C:(x + 1) * C, h, :], start=True, stop=True)
                last.then_inc(ap_done, 1)

            def reads(i, s):
                n = 2 * i + s
                e3 = hg["e3a" if s == 0 else "e3b"]
                pe.wait_ge(masked, n + 2)
                pe.wait_ge(qb_made, n + 1)
                pe.wait_ge(S1_made, n + 1)
                for h in range(H):
                    o = bank[3][:, h * P:(h + 1) * P]
                    pe.matmul(o, hg["vt"][:, h, :], hg["am"][:, h, :], start=True, stop=False)
                    pe.matmul(o[:, 0:C], hg["S0"][:, h, :], e3[:, h, 0:C], start=False, stop=False)
                    last = pe.matmul(o[:, C:P], hg["S1"][:, h, :], e3[:, h, C:P], start=False, stop=True)
                last.then_inc(o_done, 1)

            with pe.Fori(0, 4) as i:
                for s in range(2):
                    chunk(ph["gu"], i, s, 0, x_hi, x_lo)
                    turn(i, s)
                    chunk(ph["gu"], i, s, 1, x_hi, x_lo)
                    scores(i, s)
                    chunk(ph["gu"], i, s, 2, x_hi, x_lo)
                    reads(i, s)

            def mixer_end():
                pe.wait_ge(evac, ph["gu"].done + 8 * NC)
                pe.wait_ge(o_out, PAIRS + 1)
                for g in range(H):
                    last = pe.transpose(bank[3][0:23, g * P:(g + 1) * P], u_[:, g, TP - PAST:T], ident[:, :])
                last.then_inc(u_turned, 1)
                pe.wait_ge(past_in, 16)
                pe.wait_ge(masked, PAIRS + 1)
                for g in range(H):
                    last = pe.transpose(bank[5][:, g * 120:(g + 1) * 120], past[0:120, g * P:(g + 1) * P],
                                        ident[0:120, 0:120])
                last.then_inc(past_turned, 1)
                pe.wait_ge(S0_made, PAIRS + 1)

                def spread_v(b):
                    if b >= 2:
                        pe.wait_ge(new_made, 2 * (b - 2) + 1)
                    for h in range(H):
                        last = pe.matmul(bank[6 + b % 2][:, h * P:(h + 1) * P],
                                         i_[:, h, TP + b:TP + b + 1].to_broadcast([P, P]), ident[:, :],
                                         start=True, stop=True)
                    last.then_inc(v_wide, 1)

                spread_v(0)
                for b in range(NS):
                    if b + 1 < NS:
                        spread_v(b + 1)
                    pe.wait_ge(new_made, 2 * b + 2)
                    for h in range(H):
                        last = pe.matmul(bank[4][:, h * NS + b:h * NS + b + 1], s_new[b % 2][:, h, :],
                                         q_[:, h, TP + b:TP + b + 1], start=True, stop=True)
                    last.then_inc(new_read, 1)
                for h in range(H):
                    pe.wait_ge(osq_made, h + 1)
                    if h:
                        pe.wait_ge(orr_made, 2 * h)
                    for c in range(NC):
                        last = pe.matmul(bank[3 + c][:, 0:CH], ones[:, :], osq[:, c * CH:(c + 1) * CH],
                                         start=True, stop=True)
                    last.then_inc(osum, 1)
                pe.wait_ge(orr_made, 2 * H)
                pe.wait_ge(misc_in, 16)
                pe.wait_ge(spooled, 3 * H)
                for g in range(H):
                    pe.wait_ge(pooled, g + 1)
                    for c in range(NC):
                        e = 3 * g + c
                        if e >= 3:
                            pe.wait_ge(yb_made, e - 2)
                        pe.matmul(bank[3 + e % 3][:, 0:CH], pmix[:, g, :], u_[:, g, c * CH:(c + 1) * CH],
                                  start=True, stop=True).then_inc(mixed, 1)
                pe.wait_ge(ya_made, H)
                pe.wait_ge(yb_made, 3 * H)

            def norm_sums(n):
                pe.wait_ge(sq_added, 8 * NC * n)
                for c in range(NC):
                    last = pe.matmul(bank[3 + c][:, 0:CH], ones[:, :], sqacc[:, c * CH:(c + 1) * CH], start=True, stop=True)
                last.then_inc(sq_wide, 1)
                pe.wait_ge(xl_made, 8 * NC * n)

            def product(p, hi, lo, kb=KB):
                with pe.Fori(0, p.stripes // 2) as i:
                    for s in range(2):
                        for c in range(NC):
                            chunk(p, i, s, c, hi, lo, kb)

            def memory_in():
                pe.wait_ge(mem_in, 32)
                pe.wait_ge(rb_made, 3)
                for n in range(2):
                    for k in range(KB):
                        last = pe.transpose(wide(3 + 2 * n)[:, k * P:(k + 1) * P], mtok[:, n, k * P:(k + 1) * P], ident[:, :])
                    last.then_inc(mem_turned, 1)
                pe.wait_ge(mem_sq, 4)
                for n in range(2):
                    last = pe.matmul(bank[7][:, n * P:(n + 1) * P], rtok[:, 9 + n:10 + n].to_broadcast([P, P]),
                                     ident[:, :], start=True, stop=True)
                last.then_inc(rbm_wide, 1)
                pe.wait_ge(mem_step, 6)
                pe.wait_ge(evac, ph["kv"].done)

            def keys_values(p):
                with pe.Fori(0, p.stripes // 2) as i:
                    pe.wait_ge(qc_made, i + 1)
                    pe.wait_ge(ssc_made, 2 * i + 1)
                    for k in range(KB):
                        last = pe.matmul(wide(2)[:, k * P:(k + 1) * P], qcol[:, k:k + 1].to_broadcast([P, P]),
                                         ident[:, :], start=True, stop=True)
                    last.then_inc(sq_w, 1)
                    for s in range(2):
                        pe.wait_ge(lo_made, p.first + 2 * i + s + 1)
                        pe.wait_ge(evac, p.done + 2 * i + s - 1)
                        stripe_chunk(p, i, s, 0, m_hi, m_lo, cols=M, out=bank[s][:, 0:M])
                pe.wait_ge(evac, ph["co"].done)
                for x in range(4):
                    if x >= 2:
                        pe.wait_ge(kv_nat, x - 1)
                    for k in range(KB):
                        last = pe.transpose(wide(3 + 2 * (x % 2))[:, k * P:(k + 1) * P],
                                            kvT[:, 8 * (x // 2) + k, (x % 2) * P:(x % 2 + 1) * P], ident[:, :])
                    last.then_inc(kv_turned, 1)
                    if x == 1:
                        pe.wait_ge(ssc_made, 2 * NS + 1)
                        for a in range(2):
                            last = pe.transpose(bank[7][0:32, a * P:(a + 1) * P], ssc[:, a, :], ident[:, :])
                        last.then_inc(ssc_turned, 1)

            def attention():
                def scores_(n):
                    pe.wait_ge(qs_made, n + 1)
                    if not isinstance(n, int) or n:
                        pe.wait_ge(ex_made, n)
                    for h in range(H):
                        for d in range(2):
                            last = pe.matmul(wide(0)[:, h * XD:(h + 1) * XD], qs[:, 2 * h + d, :], kvT[:, 2 * h + d, :],
                                             start=(d == 0), stop=(d == 1))
                    last.then_inc(sc_done, 1)

                def turn_p(n):
                    pe.wait_ge(p_made, n + 1)
                    for h in range(H):
                        for a in range(2):
                            last = pe.transpose(wide(2)[:, (2 * h + a) * P:(2 * h + a + 1) * P], pr[:, h, a * P:(a + 1) * P],
                                                ident[:, :])
                    last.then_inc(pt_done, 1)

                def values(n):
                    pe.wait_ge(pt_out, n + 1)
                    pe.wait_ge(pv_out, n + 1)
                    for h in range(H):
                        for d in range(2):
                            for a in range(2):
                                last = pe.matmul(wide(4)[:, (2 * h + d) * P:(2 * h + d + 1) * P],
                                                 vnat[:, a, h * XD + d * P:h * XD + (d + 1) * P], prT[:, 2 * h + a, :],
                                                 start=(a == 0), stop=(a == 1))
                    last.then_inc(pv_done, 1)

                def sample_values(n, stop):
                    pe.wait_ge(spz_made, n + 1)
                    for s in range(2):
                        pe.wait_ge(vc_in[s], 16 * n + 16)
                        for d in range(2):
                            last = pe.matmul(bank[6 + d][0:NS * H, :], spz[:, s, :], vc[s][:, d * 512:(d + 1) * 512],
                                             start=False, stop=stop and s == 1)
                        last.then_inc(sv_done, 1)

                scores_(0)
                pe.wait_ge(ssm, 4)
                for a in range(2):
                    last = pe.transpose(bank[7][:, 256 + a * 32:256 + (a + 1) * 32], sp_[:, a, :], ident[0:32, 0:32])
                last.then_inc(sp_turned, 1)
                pe.wait_ge(kv_nat, 4)
                pe.wait_ge(ssm, 5)
                for d in range(2):
                    last = pe.matmul(bank[6 + d][0:NS * H, :], pad[:, 0:1].to_broadcast([P, NS * H]), rb[:, 0:512],
                                     start=True, stop=False)
                last.then_inc(sv_done, 1)
                with pe.Fori(0, PAIRS - 1) as n:
                    scores_(n + 1)
                    turn_p(n)
                    sample_values(n, False)
                    values(n)
                turn_p(PAIRS - 1)
                sample_values(NS - 1, True)
                values(PAIRS - 1)
                pe.wait_ge(so_out, 1)
                for k in range(KB):
                    last = pe.transpose(bank[0][:, k * 32:(k + 1) * 32], so[:, k * P:(k + 1) * P], ident[0:32, 0:32])
                last.then_inc(so_turned, 1)
                pe.wait_ge(so_made, 2)

            for p in phases[2:]:
                if p.name == "out":
                    mixer_end()
                    product(p, y_hi, y_lo)
                elif p.name == "cq":
                    norm_sums(1)
                    product(p, x_hi, x_lo)
                elif p.name == "kv":
                    memory_in()
                    keys_values(p)
                    attention()
                elif p.name == "co":
                    product(p, o_hi, o_lo)
                elif p.name.startswith("in"):
                    if p.name == "in0":
                        norm_sums(2)
                    product(p, x_hi, x_lo)
                else:
                    f0 = int(p.name[4:])
                    fb = dict(GROUPS)[f0]
                    pe.wait_ge(s_made, 3 * (f0 + fb))
                    product(p, s_hi, s_lo, fb)
            pe.wait_ge(evac, phases[-1].done + 8 * NC)

            def turn_y(n):
                rows = P if n < 8 else NS
                if n >= 3:
                    pe.wait_ge(y_made, n - 2)
                for k in range(KB):
                    last = pe.transpose(wide(Y_BANKS[n % 3])[0:rows, k * P:(k + 1) * P],
                                        acc[:, k, n * P:n * P + rows], ident[:, :])
                last.then_inc(y_turned, 1)

            turn_y(0)
            turn_y(1)
            pe.wait_ge(fsq_added, 8 * NC + 1)
            for n in range(9):
                rows = P if n < 8 else NS
                last = pe.matmul(bank[7][0:rows, n:n + 1], sqfin[:, n * P:n * P + rows], ones[:, 0:1],
                                 start=True, stop=True)
            last.then_inc(fsum, 1)
            for n in range(2, 9):
                turn_y(n)


INS = ["x_prompt", "x_sample", "mem_prompt", "state_hgrn", "state_pool", "cache_mem_k", "cache_mem_v", "g_mix",
       "w_in", "hgrn_lb", "hgrn_norm", "pool_mix", "pool_scale", "w_out", "g_mem", "w_mem_kv", "g_cross", "w_cq",
       "w_co", "g_ffn", "w_ffn_in", "w_ffn_out", "g_final"]
PER_LAYER = {"state_hgrn", "state_pool", "cache_mem_k", "cache_mem_v", "g_mix", "w_in", "hgrn_norm", "pool_mix",
             "pool_scale", "w_out", "g_mem", "w_mem_kv", "g_cross", "w_cq", "w_co", "g_ffn", "w_ffn_in", "w_ffn_out",
             "hgrn_prompt", "pool_prompt", "mem_k", "mem_v", "hgrn_sample", "pool_sample"}
OUTS = [("y_prompt", (1, TP, D)), ("y_sample", (NS, 1, D)), ("hgrn_prompt", (1, 1, H, P, P)),
        ("pool_prompt", (1, 1, PAST, W)), ("mem_k", (1, 1, M, H, XD)), ("mem_v", (1, 1, M, H, XD)),
        ("hgrn_sample", (1, NS, H, P, P)), ("pool_sample", (1, NS, PAST, W))]


def kernel(**inputs):
    import concourse.bacc as bacc
    from concourse.bass_utils import run_bass_kernel_spmd

    nc = bacc.Bacc("TRN2", target_bir_lowering=False, num_devices=1)
    arrays, t = {}, {}
    for name in INS:
        arrays["in_" + name] = a = np.ascontiguousarray(inputs[name])
        t[name] = nc.dram_tensor("in_" + name, a.shape, mybir.dt.from_np(a.dtype), kind="ExternalInput").ap()
    for name, shape in OUTS:
        t[name] = nc.dram_tensor("out_" + name, shape, F32, kind="ExternalOutput").ap()
    hybrid_layer(nc, t)
    r = run_bass_kernel_spmd(nc, [arrays], core_ids=[0])
    return tuple(r.results[0]["out_" + name] for name, _ in OUTS)
```
